# Optimizing a Trainium2 kernel written in Bass

```python
import math
import jax, jax.numpy as jnp
from jax import lax
import numpy as np

D_MODEL = 1024
BATCH = 1
SEQ = 256
DEPTH = 2

HEAD_DIM = 64
N_HEADS = D_MODEL // HEAD_DIM
A_HEADS = 4
B_HEADS = 6
C_HEADS = N_HEADS - A_HEADS - B_HEADS
A_WIDTH = A_HEADS * HEAD_DIM
B_WIDTH = B_HEADS * HEAD_DIM
C_WIDTH = C_HEADS * HEAD_DIM
A_QK_DIM = HEAD_DIM // 2
ROPE_THETA = 500000.0
ROPE_FRACTION = 4
DILATED_BRANCHES = ((128, 1), (512, 4), (2048, 16))
DENSE_Q_BLOCK = 128
MOBA_BLOCK = 256
MOBA_TOP_K = 3
MOBA_Q_CHUNK = 16
MEM_LEN = 256
MEM_HEADS = 4
MEM_HEAD_DIM = 64
MEM_WIDTH = MEM_HEADS * MEM_HEAD_DIM
D_FF = 2816
NORM_EPS = 1e-6
NEG_INF = -1e30
POS_OFFSET_MAX = 4096

kernel_name = "hymba_style_diff_dilated_moba_macaron"

def rms_norm(x, g):
    xf = x.astype(jnp.float32)
    y = xf * lax.rsqrt(jnp.mean(xf * xf, axis=-1, keepdims=True) + NORM_EPS)
    return (y * g.astype(jnp.float32)).astype(x.dtype)

def swiglu(h, w_gate, w_up, w_down):
    return (jax.nn.silu(h @ w_gate) * (h @ w_up)) @ w_down

def rotary_tables(positions, rot_dim):
    inv_freq = ROPE_THETA ** (-jnp.arange(0, rot_dim, 2, dtype=jnp.float32) / rot_dim)
    ang = positions.astype(jnp.float32)[..., None] * inv_freq
    return jnp.cos(ang), jnp.sin(ang)

def apply_partial_rotary(x, cos, sin):
    r = 2 * cos.shape[-1]
    c = cos[:, :, None, :].astype(x.dtype)
    s = sin[:, :, None, :].astype(x.dtype)
    x1, x2, xp = x[..., : r // 2], x[..., r // 2: r], x[..., r:]
    return jnp.concatenate([x1 * c - x2 * s, x2 * c + x1 * s, xp], axis=-1)

def differential_attention(q, k, v, lam, subln_g, lam_init):
    S = q.shape[1]
    dq = q.shape[-1] // 2
    scale = dq ** -0.5
    q1, q2 = q[..., :dq] * scale, q[..., dq:] * scale
    k1, k2 = k[..., :dq], k[..., dq:]
    outs = []
    for i in range(S // DENSE_Q_BLOCK):
        q_lo, q_hi = i * DENSE_Q_BLOCK, (i + 1) * DENSE_Q_BLOCK
        mask = jnp.arange(q_hi)[None, :] <= jnp.arange(q_lo, q_hi)[:, None]
        s1 = jnp.einsum('bqhd,bkhd->bhqk', q1[:, q_lo:q_hi], k1[:, :q_hi]).astype(jnp.float32)
        s2 = jnp.einsum('bqhd,bkhd->bhqk', q2[:, q_lo:q_hi], k2[:, :q_hi]).astype(jnp.float32)
        p1 = jax.nn.softmax(jnp.where(mask, s1, NEG_INF), axis=-1)
        p2 = jax.nn.softmax(jnp.where(mask, s2, NEG_INF), axis=-1)
        a = (p1 - lam * p2).astype(v.dtype)
        outs.append(jnp.einsum('bhqk,bkhd->bqhd', a, v[:, :q_hi]))
    o = jnp.concatenate(outs, axis=1)
    return rms_norm(o, subln_g) * (1.0 - lam_init)

def dilated_branch(q, k, v, window, dilation):
    B_, S, H, dh = q.shape
    L = S // dilation
    span = window // dilation
    Lp = -(-L // span) * span
    nb = Lp // span

    def to_sub(t):
        t = t.reshape(B_, L, dilation, H, dh).transpose(0, 2, 3, 1, 4)
        t = jnp.pad(t, ((0, 0), (0, 0), (0, 0), (0, Lp - L), (0, 0)))
        return t.reshape(B_, dilation, H, nb, span, dh)

    qb = to_sub(q) * dh ** -0.5
    kb, vb = to_sub(k), to_sub(v)
    prev = lambda t: jnp.pad(t, ((0, 0), (0, 0), (0, 0), (1, 0), (0, 0), (0, 0)))[:, :, :, :-1]
    kk = jnp.concatenate([prev(kb), kb], axis=4)
    vv = jnp.concatenate([prev(vb), vb], axis=4)
    s = jnp.einsum('brhnqd,brhnkd->brhnqk', qb, kk).astype(jnp.float32)
    qi = jnp.arange(span)[:, None] + span
    ki = jnp.arange(2 * span)[None, :]
    rel = qi - ki
    band = (rel >= 0) & (rel <= span)
    has_prev = (jnp.arange(nb) > 0)[:, None, None] | (ki >= span)[None]
    s = jnp.where(band[None] & has_prev, s, NEG_INF)
    lse = jax.nn.logsumexp(s, axis=-1)
    p = jnp.exp(s - lse[..., None]).astype(v.dtype)
    o = jnp.einsum('brhnqk,brhnkd->brhnqd', p, vv)
    o = o.reshape(B_, dilation, H, Lp, dh)[:, :, :, :L].transpose(0, 3, 1, 2, 4).reshape(B_, S, H, dh)
    lse = lse.reshape(B_, dilation, H, Lp)[..., :L].transpose(0, 3, 1, 2).reshape(B_, S, H)
    return o, lse

def dilated_attention(q, k, v):
    outs, lses = [], []
    for window, dilation in DILATED_BRANCHES:
        o, lse = dilated_branch(q, k, v, window, dilation)
        outs.append(o)
        lses.append(lse)
    w = jax.nn.softmax(jnp.stack(lses, axis=0), axis=0)
    o = jnp.einsum('nbsh,nbshd->bshd', w, jnp.stack(outs, axis=0).astype(jnp.float32))
    return o.astype(q.dtype)

def moba_attention(q, k, v):
    B_, S, H, dh = q.shape
    nblk = -(-S // MOBA_BLOCK)
    Sp = nblk * MOBA_BLOCK

    def prep(t):
        return jnp.pad(t, ((0, 0), (0, Sp - S), (0, 0), (0, 0))).transpose(0, 2, 1, 3)

    qh = prep(q) * dh ** -0.5
    kh, vh = prep(k), prep(v)
    qb = qh.reshape(B_, H, nblk, MOBA_BLOCK, dh)
    kb = kh.reshape(B_, H, nblk, MOBA_BLOCK, dh)
    vb = vh.reshape(B_, H, nblk, MOBA_BLOCK, dh)

    s_own = jnp.einsum('bhnqd,bhnkd->bhnqk', qb, kb).astype(jnp.float32)
    causal = jnp.tril(jnp.ones((MOBA_BLOCK, MOBA_BLOCK), dtype=bool))
    s_own = jnp.where(causal, s_own, NEG_INF)
    lse_own = jax.nn.logsumexp(s_own, axis=-1)
    o_own = jnp.einsum('bhnqk,bhnkd->bhnqd', jnp.exp(s_own - lse_own[..., None]).astype(v.dtype), vb)
    o_own = o_own.reshape(B_, H, Sp, dh)
    lse_own = lse_own.reshape(B_, H, Sp)

    k_mean = jnp.mean(kb.astype(jnp.float32), axis=3)
    gate = jnp.einsum('bhsd,bhnd->bhsn', qh.astype(jnp.float32), k_mean)
    q_blk = jnp.arange(Sp) // MOBA_BLOCK
    is_past = jnp.arange(nblk)[None, :] < q_blk[:, None]
    gate = jnp.where(is_past, gate, -jnp.inf)
    n_sel = min(MOBA_TOP_K, nblk)
    _, sel = lax.top_k(gate, n_sel)
    sel_ok = sel < q_blk[:, None]

    n_chunks = Sp // MOBA_Q_CHUNK

    def chunks(t):
        return jnp.moveaxis(t.reshape(B_, H, n_chunks, MOBA_Q_CHUNK, *t.shape[3:]), 2, 0)

    bi = jnp.arange(B_)[:, None, None, None]
    hi = jnp.arange(H)[None, :, None, None]

    def attend_selected(args):
        qc, sc, okc = args
        kg = kb[bi, hi, sc]
        vg = vb[bi, hi, sc]
        s = jnp.einsum('bhqd,bhqnkd->bhqnk', qc, kg).astype(jnp.float32)
        s = jnp.where(okc[..., None], s, NEG_INF).reshape(B_, H, MOBA_Q_CHUNK, n_sel * MOBA_BLOCK)
        lse = jax.nn.logsumexp(s, axis=-1)
        p = jnp.exp(s - lse[..., None]).reshape(B_, H, MOBA_Q_CHUNK, n_sel, MOBA_BLOCK)
        o = jnp.einsum('bhqnk,bhqnkd->bhqd', p.astype(vg.dtype), vg)
        return o, lse

    o_sel, lse_sel = lax.map(attend_selected, (chunks(qh), chunks(sel), chunks(sel_ok)))
    o_sel = jnp.moveaxis(o_sel, 0, 2).reshape(B_, H, Sp, dh)
    lse_sel = jnp.moveaxis(lse_sel, 0, 2).reshape(B_, H, Sp)

    m = jnp.maximum(lse_own, lse_sel)
    w_own = jnp.exp(lse_own - m)[..., None]
    w_sel = jnp.exp(lse_sel - m)[..., None]
    o = (w_own * o_own.astype(jnp.float32) + w_sel * o_sel.astype(jnp.float32)) / (w_own + w_sel)
    return o.astype(q.dtype).transpose(0, 2, 1, 3)[:, :S]

def memory_cross_attention(h, m, w_q, w_kv, w_o):
    B_, S, _ = h.shape
    M = m.shape[1]
    q = (h @ w_q).reshape(B_, S, MEM_HEADS, MEM_HEAD_DIM) * MEM_HEAD_DIM ** -0.5
    kv = (m @ w_kv).reshape(B_, M, 2, MEM_HEADS, MEM_HEAD_DIM)
    k, v = kv[:, :, 0], kv[:, :, 1]
    s = jnp.einsum('bshd,bmhd->bhsm', q, k).astype(jnp.float32)
    p = jax.nn.softmax(s, axis=-1).astype(v.dtype)
    o = jnp.einsum('bhsm,bmhd->bshd', p, v).reshape(B_, S, MEM_WIDTH)
    return o @ w_o

def setup_inputs(seed: int = 0) -> dict:
    key = jax.random.key(seed)
    ks = iter(jax.random.split(key, 40))
    L, D, F = DEPTH, D_MODEL, D_FF

    def nrm(shape, fan_in):
        return jax.random.normal(next(ks), shape, jnp.float32) * fan_in ** -0.5

    def gain(shape):
        return 1.0 + 0.01 * jax.random.normal(next(ks), shape, jnp.float32)

    x = jax.random.normal(next(ks), (BATCH, SEQ, D), jnp.float32)
    mem = jax.random.normal(next(ks), (BATCH, MEM_LEN, D), jnp.float32)
    positions = (jnp.arange(SEQ, dtype=jnp.int32)[None, :]
                 + jax.random.randint(next(ks), (BATCH, 1), 0, POS_OFFSET_MAX, dtype=jnp.int32))
    return {
        "x": x,
        "mem": mem,
        "positions": positions,
        "ffn1_norm": gain((L, D)),
        "ffn1_w_gate": nrm((L, D, F), D),
        "ffn1_w_up": nrm((L, D, F), D),
        "ffn1_w_down": nrm((L, F, D), F),
        "mix_norm": gain((L, D)),
        "w_in": nrm((L, D, 3 * D), D),
        "w_out": nrm((L, D, D), D),
        "diff_lambda_q1": 0.1 * jax.random.normal(next(ks), (L, A_QK_DIM), jnp.float32),
        "diff_lambda_k1": 0.1 * jax.random.normal(next(ks), (L, A_QK_DIM), jnp.float32),
        "diff_lambda_q2": 0.1 * jax.random.normal(next(ks), (L, A_QK_DIM), jnp.float32),
        "diff_lambda_k2": 0.1 * jax.random.normal(next(ks), (L, A_QK_DIM), jnp.float32),
        "diff_subln": gain((L, HEAD_DIM)),
        "memq_norm": gain((L, D)),
        "memkv_norm": gain((L, D)),
        "mem_w_q": nrm((L, D, MEM_WIDTH), D),
        "mem_w_kv": nrm((L, D, 2 * MEM_WIDTH), D),
        "mem_w_o": nrm((L, MEM_WIDTH, D), MEM_WIDTH),
        "ffn2_norm": gain((L, D)),
        "ffn2_w_gate": nrm((L, D, F), D),
        "ffn2_w_up": nrm((L, D, F), D),
        "ffn2_w_down": nrm((L, F, D), F),
        "final_norm": gain((D,)),
    }

def reference(x, mem, positions, ffn1_norm, ffn1_w_gate, ffn1_w_up, ffn1_w_down, mix_norm, w_in, w_out,
              diff_lambda_q1, diff_lambda_k1, diff_lambda_q2, diff_lambda_k2, diff_subln,
              memq_norm, memkv_norm, mem_w_q, mem_w_kv, mem_w_o,
              ffn2_norm, ffn2_w_gate, ffn2_w_up, ffn2_w_down, final_norm):
    B_, S, D = x.shape
    cos_a, sin_a = rotary_tables(positions, A_QK_DIM // ROPE_FRACTION)
    cos_h, sin_h = rotary_tables(positions, HEAD_DIM // ROPE_FRACTION)
    widths = (A_WIDTH, A_WIDTH, A_WIDTH, B_WIDTH, B_WIDTH, B_WIDTH, C_WIDTH, C_WIDTH, C_WIDTH)
    split_at = [sum(widths[:i + 1]) for i in range(len(widths) - 1)]

    for l in range(DEPTH):
        lam_init = 0.8 - 0.6 * math.exp(-0.3 * l)

        x = x + 0.5 * swiglu(rms_norm(x, ffn1_norm[l]), ffn1_w_gate[l], ffn1_w_up[l], ffn1_w_down[l])

        h = rms_norm(x, mix_norm[l])
        qa, ka, va, qb, kb, vb, qc, kc, vc = jnp.split(h @ w_in[l], split_at, axis=-1)

        qa = apply_partial_rotary(qa.reshape(B_, S, 2 * A_HEADS, A_QK_DIM), cos_a, sin_a).reshape(B_, S, A_HEADS, HEAD_DIM)
        ka = apply_partial_rotary(ka.reshape(B_, S, 2 * A_HEADS, A_QK_DIM), cos_a, sin_a).reshape(B_, S, A_HEADS, HEAD_DIM)
        va = va.reshape(B_, S, A_HEADS, HEAD_DIM)
        lam = (jnp.exp(jnp.sum(diff_lambda_q1[l].astype(jnp.float32) * diff_lambda_k1[l].astype(jnp.float32)))
               - jnp.exp(jnp.sum(diff_lambda_q2[l].astype(jnp.float32) * diff_lambda_k2[l].astype(jnp.float32)))
               + lam_init)
        o_a = differential_attention(qa, ka, va, lam, diff_subln[l], lam_init)

        qb = apply_partial_rotary(qb.reshape(B_, S, B_HEADS, HEAD_DIM), cos_h, sin_h)
        kb = apply_partial_rotary(kb.reshape(B_, S, B_HEADS, HEAD_DIM), cos_h, sin_h)
        o_b = dilated_attention(qb, kb, vb.reshape(B_, S, B_HEADS, HEAD_DIM))

        qc = apply_partial_rotary(qc.reshape(B_, S, C_HEADS, HEAD_DIM), cos_h, sin_h)
        kc = apply_partial_rotary(kc.reshape(B_, S, C_HEADS, HEAD_DIM), cos_h, sin_h)
        o_c = moba_attention(qc, kc, vc.reshape(B_, S, C_HEADS, HEAD_DIM))

        mixed = jnp.concatenate([o_a.reshape(B_, S, A_WIDTH), o_b.reshape(B_, S, B_WIDTH),
                                 o_c.reshape(B_, S, C_WIDTH)], axis=-1)
        x = x + mixed @ w_out[l]

        x = x + memory_cross_attention(rms_norm(x, memq_norm[l]), rms_norm(mem, memkv_norm[l]),
                                       mem_w_q[l], mem_w_kv[l], mem_w_o[l])

        x = x + 0.5 * swiglu(rms_norm(x, ffn2_norm[l]), ffn2_w_gate[l], ffn2_w_up[l], ffn2_w_down[l])

    return rms_norm(x, final_norm)


_drawn_inputs = setup_inputs


def setup_inputs(seed=0):
    import zlib

    import numpy as np

    out = dict(_drawn_inputs(seed))
    spreads = {}
    factors = {'ffn1_norm': 8.0,
     'mix_norm': 5.772,
     'diff_subln': 34.508,
     'memq_norm': 8.0,
     'memkv_norm': 8.0,
     'ffn2_norm': 8.0,
     'final_norm': 32.618}
    for name, (base, spread) in spreads.items():
        noise = np.random.default_rng([zlib.crc32(name.encode()), seed]).standard_normal(out[name].shape)
        drawn = base * np.exp(spread * noise) if base else spread * noise
        out[name] = __import__('jax').numpy.asarray(drawn.astype(out[name].dtype))
    for name, factor in factors.items():
        out[name] = (out[name] * factor).astype(out[name].dtype)
    return out
```

```python
import math
from contextlib import ExitStack

import numpy as np

import concourse.bass as bass
from concourse import mybir

F32 = mybir.dt.float32
F32R = mybir.dt.float32r
BF16 = mybir.dt.bfloat16
I32 = mybir.dt.int32
ALU = mybir.AluOpType
ACT = mybir.ActivationFunctionType
AX = mybir.AxisListType

P = 128
D = 1024
SEQ = 256
MEM = 256
DEPTH = 2
FF = 2816
HD = 64
A_HEADS, B_HEADS, C_HEADS = 4, 6, 6
A_MAP = HD // 2
MEM_HEADS = 4
EPS = 1e-6
NEG = -1e30
BIG = 3e38
ROPE_THETA = 500000.0
BRANCHES = ((128, 1), (512, 4), (2048, 16))

TT = SEQ // P
KC = D // P
PIECE = 1024
RING = 6
RAW = 3
STEPS = FF // 256
HALF = 512

AQ, AK, AV = 0, 256, 512
BQ, BK, BV = 768, 1152, 1536
CQ, CK, CV = 1920, 2304, 2688
BLOCKS = 3 * D // HALF
PLACES = 6

P_FFN = 6 * STEPS
P_IN, P_KV, P_OUT, P_MQ, P_MO = P_FFN, P_FFN + 24, P_FFN + 28, P_FFN + 36, P_FFN + 38
P_FFN2 = P_FFN + 40
P_LAYER = P_FFN2 + P_FFN
PIECES = DEPTH * P_LAYER

T_FFN1, T_MIX, T_OUT, T_MQ, T_MO, T_FFN2, T_LAYER = 0, 4, 8, 12, 16, 17, 21
X_FFN1, X_OUT, X_MO, X_FFN2, X_LAYER = 0, 4, 8, 12, 16

ROT, ROT_A = HD // 4, A_MAP // 4
NF = ROT // 2 + ROT_A // 2

N_PARAMS = 1 + TT + 5 * DEPTH + 4 + 1

K_CAUSAL, K_DILATED, K_ZERO, K_ID, K_ONE, K_FREQ = 0, 384, 768, 1024, 1152, 1280
K_COLS = K_FREQ + NF


def shape_constants():
    out = np.zeros((P, K_COLS), np.float32)
    for tile, first, keys in ((0, 0, 128), (1, 128, 256)):
        delta = (tile * P + np.arange(P))[:, None] - np.arange(keys)[None, :]
        count = np.zeros(delta.shape)
        for window, dilation in BRANCHES:
            count += (delta >= 0) & (delta % dilation == 0) & (delta <= window)
        out[:, K_CAUSAL + first:K_CAUSAL + first + keys] = np.where(delta >= 0, 0.0, NEG)
        out[:, K_DILATED + first:K_DILATED + first + keys] = np.where(
            count > 0, math.sqrt(HD) * np.log(np.maximum(count, 1)), NEG)
    out[:, K_ID:K_ID + P] = np.eye(P)
    out[:, K_ONE:K_ONE + P] = 1.0
    theta = np.float32(ROPE_THETA)
    for at, rot in ((0, ROT), (ROT // 2, ROT_A)):
        out[:, K_FREQ + at:K_FREQ + at + rot // 2] = theta ** (-np.arange(0, rot, 2, dtype=np.float32) / np.float32(rot))
    return out


class Head:

    def __init__(self, group, h, maps, v_col, mask, batch, slot, last):
        self.group, self.h, self.maps, self.v_col, self.mask = group, h, maps, v_col, mask
        self.batch, self.slot, self.last = batch, slot, last


def heads_of(group):
    out = []
    if group == "a":
        for h in range(A_HEADS):
            maps = [((2 * h + j) // 4, 2 + (2 * h + j) // 4, 32 * ((2 * h + j) % 4), 32) for j in (0, 1)]
            out.append(Head(group, h, maps, AV + h * HD, K_CAUSAL, 4, h, h == 3))
    elif group in "bc":
        q0, k0, v0 = (4, 7, BV) if group == "b" else (10, 13, CV)
        mask = K_DILATED if group == "b" else K_CAUSAL
        for h in range(B_HEADS):
            out.append(Head(group, h, [(q0 + h // 2, k0 + h // 2, 64 * (h % 2), 64)],
                            v0 + h * HD, mask, 3, h % 3, h % 3 == 2))
    else:
        for h in range(MEM_HEADS):
            out.append(Head(group, h, [(h // 2, h // 2, 64 * (h % 2), 64)], h * HD, K_ZERO, 4, h, h == 3))
    return out


def attention_events(groups):
    heads = [h for g in groups for h in heads_of(g)]
    out = []
    for i in range(len(heads) + 3):
        if i < len(heads):
            out.append(("scores", heads[i]))
        if 0 <= i - 2 < len(heads):
            out.append(("turn", heads[i - 2]))
        if 0 <= i - 3 < len(heads):
            out.append(("apply", heads[i - 3]))
    return out


def mix_events():
    turns = {"a": [0, 1], "b": [2, 3, 4], "c": [5, 6, 7]}
    out = []
    for b in range(BLOCKS):
        out.append(("block", b))
    for g in "abc":
        out.append(("rotate", g))
        out += [("turn_qk", p) for p in turns[g]]
    out += [("mem_kv", 0)]
    out += attention_events("abc")
    return out


def number_events():
    count = {"map": 0, "head": 0, "batch": 0, "qk": 0, "rot": 0}
    layers = []
    for _ in range(DEPTH):
        parts = []
        for events in (mix_events(), attention_events("m")):
            part = []
            for what, arg in events:
                n = {}
                if what == "scores":
                    n = {"map": count["map"], "slot": count["map"]}
                    arg_maps = len(arg.maps)
                    count["map"] += arg_maps
                elif what == "turn_qk":
                    n = {"qk": count["qk"]}
                    count["qk"] += 1
                elif what == "rotate":
                    n = {"rot": count["rot"]}
                    count["rot"] += 1
                part.append([what, arg, n])
            seen = {}
            order = [e for e in part if e[0] == "scores"]
            for e in order:
                seen[id(e[1])] = {"map": e[2]["map"], "head": count["head"], "batch": count["batch"]}
                count["head"] += 1
                count["batch"] += e[1].last
            for e in part:
                if e[0] in ("scores", "turn", "apply"):
                    e[2] = seen[id(e[1])]
            parts.append(part)
        layers.append(parts)
    return layers


def decoder_trunk(nc, t, constants, out):
    layers = number_events()
    with ExitStack() as ctx:
        def sb(name, shape, dt=F32):
            return ctx.enter_context(nc.sbuf_tensor(name, shape, dt))

        def sem(name):
            return ctx.enter_context(nc.semaphore(name))

        x_rows = sb("x_rows", [P, TT, D])
        w_raw = sb("w_raw", [P, RAW, PIECE])
        w_hi = sb("w_hi", [P, RING, PIECE], F32R)
        w_lo = sb("w_lo", [P, RING, PIECE], F32R)
        c_hi = sb("c_hi", [P, KC, SEQ], F32R)
        c_lo = sb("c_lo", [P, KC, SEQ], F32R)
        mem_cols = sb("mem_cols", [P, KC, MEM])
        m_hi = sb("m_hi", [P, KC, MEM], F32R)
        m_lo = sb("m_lo", [P, KC, MEM], F32R)
        mem_k = sb("mem_k", [P, 2, MEM])
        mem_q = sb("mem_q", [P, 2, SEQ])
        mem_v = sb("mem_v", [P, TT, MEM_HEADS * HD])
        qkv = sb("qkv", [P, TT, 3 * D])
        qk_cols = sb("qk_cols", [P, 16, SEQ])
        mixed = sb("mixed", [P, TT, D])
        probs = sb("probs", [P, PLACES, HALF])
        probs_t = sb("probs_t", [P, 2, HALF])
        bias = sb("bias", [P, PLACES, TT])
        sums = sb("sums", [P, 2, TT, 4, 2])
        recips = sb("recips", [P, 2, TT, 4, 2])
        out_a = sb("out_a", [P, TT, A_HEADS, HD])
        sq_a = sb("sq_a", [P, TT, A_HEADS, HD])
        rms_a = sb("rms_a", [P, 4, TT * A_HEADS])
        rot_1 = sb("rot_1", [P, TT, 2 * B_HEADS * ROT])
        rot_2 = sb("rot_2", [P, TT, 2 * B_HEADS * ROT])
        gate = sb("gate", [P, HALF])
        hidden = sb("hidden", [P, HALF])
        h_hi = sb("h_hi", [P, HALF], F32R)
        h_lo = sb("h_lo", [P, HALF], F32R)
        squares = sb("squares", [P, D], BF16)
        rms = sb("rms", [P, 4, TT])
        rms_scaled = sb("rms_scaled", [P, TT])
        diag = sb("diag", [P, TT, P])
        rms_cols = sb("rms_cols", [P, SEQ])
        const = sb("const", [P, K_COLS])
        gain_rows = sb("gain_rows", [10 * KC, P])
        gains = sb("gains", [P, 10 * KC])
        final_gain = qk_cols[:, 0:D // SEQ, :].rearrange("p k n -> p (k n)")
        lambdas = sb("lambdas", [P, 4, DEPTH, A_MAP])
        lam = sb("lam", [P, 4, DEPTH, 2])
        subln = sb("subln", [P, DEPTH, HD])
        pos = sb("pos", [P, TT], I32)
        pos_f = sb("pos_f", [P, TT])
        angle = sb("angle", [P, 4, 2, TT, NF])
        cos_h = sb("cos_h", [P, TT, ROT])
        sin_h = sb("sin_h", [P, TT, ROT])
        cos_a = sb("cos_a", [P, TT, ROT_A])
        sin_a = sb("sin_a", [P, TT, ROT_A])

        ident = const[:, K_ID:K_ID + P]
        bank = [ctx.enter_context(nc.psum_tensor(f"bank{i}", [P, HALF], F32)) for i in range(8)]
        GATE, UP = 4, 5

        params_loaded = sem("params_loaded")
        x_loaded = sem("x_loaded")
        mem_loaded = sem("mem_loaded")
        weights_loaded = [sem(f"weights_loaded{i}") for i in range(RAW)]
        pieces_rounded = sem("pieces_rounded")
        pieces_split = sem("pieces_split")
        pieces_used = sem("pieces_used")
        vector_done = sem("vector_done")
        pool_done = sem("pool_done")
        gains_turned = sem("gains_turned")
        gains_ready = sem("gains_ready")
        lambdas_summed = sem("lambdas_summed")
        lambdas_exp = sem("lambdas_exp")
        angles_ready = sem("angles_ready")
        sines_ready = sem("sines_ready")
        tables_ready = sem("tables_ready")
        mem_squared = sem("mem_squared")
        mem_scaled = sem("mem_scaled")
        mem_turned = sem("mem_turned")
        mem_cols_ready = sem("mem_cols_ready")
        mem_rounded = sem("mem_rounded")
        mem_split = sem("mem_split")
        x_updated = sem("x_updated")
        x_squared = sem("x_squared")
        rms_ready = sem("rms_ready")
        diag_ready = sem("diag_ready")
        rms_spread = sem("rms_spread")
        rms_cols_ready = sem("rms_cols_ready")
        cols_turned = sem("cols_turned")
        cols_rounded = sem("cols_rounded")
        cols_split = sem("cols_split")
        gates_scaled = sem("gates_scaled")
        gates_active = sem("gates_active")
        hidden_ready = sem("hidden_ready")
        hidden_rounded = sem("hidden_rounded")
        hidden_split = sem("hidden_split")
        rows0_stored = sem("rows0_stored")
        rows1_stored = sem("rows1_stored")
        rotated = sem("rotated")
        qk_turned = sem("qk_turned")
        qk_stored = sem("qk_stored")
        mem_k_stored = sem("mem_k_stored")
        mem_v_stored = sem("mem_v_stored")
        mem_q_stored = sem("mem_q_stored")
        scored = sem("scored")
        masked = sem("masked")
        exped = sem("exped")
        combined = sem("combined")
        probs_turned = sem("probs_turned")
        probs_stored = sem("probs_stored")
        applied = sem("applied")
        mixed_stored = sem("mixed_stored")
        final_loaded = sem("final_loaded")
        out_ready = sem("out_ready")
        out_stored = sem("out_stored")

        def raw(view):
            return view.bitcast(F32)

        def gain_col(layer, which, kc):
            at = (layer * 5 + which) * KC + kc
            return gains[:, at:at + 1]

        def kind_of_ffn(f):
            return f // 2, f % 2

        def ffn_piece(f):
            layer, which = kind_of_ffn(f)
            return layer * P_LAYER + which * P_FFN2

        place_free = {}
        owner = {e[2]["map"] + j: e[2]["head"] for parts in layers for part in parts for e in part
                 if e[0] == "scores" for j in range(len(e[1].maps))}
        owner_heads = set(owner.values())
        for m in owner:
            if m >= PLACES:
                place_free[m] = owner[m - PLACES] + 1

        block = ctx.enter_context(nc.Block())

        @block.sync
        def _(sp):
            def load_piece(n, i, source):
                slot = n % RAW
                if n >= RAW:
                    sp.wait_ge(pieces_split, n - RAW + 1 + RING * i)
                sp.dma_start(w_raw[:, slot, :].rearrange("p (k n) -> p k n", n=source.shape[-1]),
                             source).then_inc(weights_loaded[slot], 16)

            def up_source(w, half, i):
                view = w.rearrange("(h k p) f -> p h k f", h=2, p=P)
                return view[:, half, :, bass.ds(i * 256, 256)]

            def down_source(w, half, i):
                view = w.rearrange("(c h p) n -> p c h n", h=2, p=P)
                return view[:, bass.ds(i, 1), half, :]

            def load_ffn(f):
                layer, which = kind_of_ffn(f)
                name = "ffn1" if which == 0 else "ffn2"
                wg, wu, wd = (t[f"{name}_w_{x}"][layer] for x in ("gate", "up", "down"))
                base = ffn_piece(f)

                for j, source in enumerate((up_source(wg, 0, 0), up_source(wg, 1, 0),
                                            up_source(wu, 0, 0), up_source(wu, 1, 0))):
                    load_piece(base + j, 0, source)
                with sp.Fori(0, STEPS - 1) as i:
                    for j, source in enumerate((up_source(wg, 0, i + 1), up_source(wg, 1, i + 1),
                                                up_source(wu, 0, i + 1), up_source(wu, 1, i + 1),
                                                down_source(wd, 0, i), down_source(wd, 1, i))):
                        load_piece(base + 4 + j, i, source)
                load_piece(base + P_FFN - 2, 0, down_source(wd, 0, STEPS - 1))
                load_piece(base + P_FFN - 1, 0, down_source(wd, 1, STEPS - 1))

            def load_rest(layer):
                n = layer * P_LAYER
                w_in = t["w_in"][layer].rearrange("(j k p) n -> p j k n", k=2, p=P)
                for b in range(BLOCKS):
                    for j in range(4):
                        load_piece(n + P_IN + 4 * b + j, 0, w_in[:, j, :, b * HALF:(b + 1) * HALF])
                kv = t["mem_w_kv"][layer].rearrange("(h k p) n -> p h k n", h=2, p=P)
                for j in range(4):
                    load_piece(n + P_KV + j, 0, kv[:, j % 2, :, (j // 2) * 256:(j // 2 + 1) * 256])
                w_out = t["w_out"][layer].rearrange("(k p) n -> p k n", p=P)
                for j in range(8):
                    load_piece(n + P_OUT + j, 0, w_out[:, j:j + 1, :])
                wq = t["mem_w_q"][layer].rearrange("(h k p) n -> p h k n", h=2, p=P)
                for j in range(2):
                    load_piece(n + P_MQ + j, 0, wq[:, j, :, :])
                wo = t["mem_w_o"][layer].rearrange("(k p) n -> p k n", p=P)
                for j in range(2):
                    load_piece(n + P_MO + j, 0, wo[:, j:j + 1, :])

            sp.dma_start(x_rows[:, :, :], t["x"][0].rearrange("(t p) d -> p t d", p=P)).then_inc(x_loaded, 16)
            for layer in range(DEPTH):
                load_ffn(2 * layer)
                load_rest(layer)
                load_ffn(2 * layer + 1)
            sp.wait_ge(applied, len(owner_heads))
            sp.dma_start(final_gain, t["final_norm"].partition_broadcast(P)).then_inc(final_loaded, 16)
            for tt in range(TT):
                sp.wait_ge(out_ready, tt + 1)
                sp.dma_start(out[0, tt * P:(tt + 1) * P, :], x_rows[:, tt, :]).then_inc(out_stored, 16)
            sp.wait_ge(out_stored, 16 * TT)

        @block.gpsimd
        def _(pool):
            count = [0]

            def link(ins):
                count[0] += 1
                ins.then_inc(pool_done, 1)
                pool.wait_ge(pool_done, count[0])

            def load(to, source, signal=params_loaded):
                pool.dma_start(to, source).then_inc(signal, 16)

            load(const[:, :], constants)
            for tt in range(TT):
                load(pos[:, tt:tt + 1], t["positions"][0, tt * P:(tt + 1) * P].unsqueeze(1))
            for layer in range(DEPTH):
                for which, name in enumerate(("ffn1_norm", "mix_norm", "memq_norm", "memkv_norm", "ffn2_norm")):
                    at = (layer * 5 + which) * KC
                    load(gain_rows[at:at + KC, :], t[name][layer].rearrange("(k p) -> k p", p=P))
            for j, name in enumerate(("q1", "k1", "q2", "k2")):
                load(lambdas[:, j, :, :].rearrange("p l d -> p (l d)"),
                     t[f"diff_lambda_{name}"].rearrange("l d -> (l d)").partition_broadcast(P))
            load(subln[:, :, :].rearrange("p l d -> p (l d)"),
                 t["diff_subln"].rearrange("l d -> (l d)").partition_broadcast(P))
            load(mixed[:, :, :], t["mem"][0].rearrange("(t p) d -> p t d", p=P), mem_loaded)

            for layer in range(DEPTH):
                for what, arg, n in layers[layer][0]:
                    if what != "rotate":
                        continue
                    first, heads, wide, rot, cos, sin, blocks = {
                        "a": (AQ, 4 * A_HEADS, A_MAP, ROT_A, cos_a, sin_a, 1),
                        "b": (BQ, 2 * B_HEADS, HD, ROT, cos_h, sin_h, 3),
                        "c": (CQ, 2 * C_HEADS, HD, ROT, cos_h, sin_h, 6)}[arg]
                    if layer == 0 and arg == "a":
                        pool.wait_ge(tables_ready, 1)
                    pool.wait_ge(rows0_stored, layer * BLOCKS + blocks)
                    pool.wait_ge(rows1_stored, layer * BLOCKS + blocks)
                    h = rot // 2
                    for tt in range(TT):
                        rows = qkv[:, tt, first:first + heads * wide].rearrange("p (h d) -> p h d", d=wide)
                        t1, t2 = (r[:, tt, 0:heads * rot].rearrange("p (h d) -> p h d", d=rot) for r in (rot_1, rot_2))
                        c = cos[:, tt, :].unsqueeze(1).broadcast_to([P, heads, rot])
                        s = sin[:, tt, :].unsqueeze(1).broadcast_to([P, heads, rot])
                        pool.tensor_tensor(t1, rows[:, :, 0:rot], c, ALU.mult)
                        pool.tensor_tensor(t2[:, :, 0:h], rows[:, :, h:rot], s[:, :, 0:h], ALU.mult)
                        link(pool.tensor_tensor(t2[:, :, h:rot], rows[:, :, 0:h], s[:, :, h:rot], ALU.mult))
                        last = pool.tensor_tensor(rows[:, :, 0:rot], t1, t2, ALU.add)
                        if tt < TT - 1:
                            link(last)
                    last.then_inc(rotated, 1)

        @block.scalar
        def _(act):
            def prepare(n, i=0):
                if isinstance(n, int) and n >= PIECES:
                    return
                slot = n % RING
                act.wait_ge(weights_loaded[n % RAW], 16 * (n // RAW + 1) + 16 * (RING // RAW) * i)
                if n >= RING:
                    act.wait_ge(pieces_used, n - RING + 1 + RING * i)
                act.activation(w_hi[:, slot, :], w_raw[:, n % RAW, :], ACT.Copy).then_inc(pieces_rounded, 1)

            def ahead(n, count=1, i=0):
                for k in range(count):
                    prepare(n + k + RING, i)

            def square(instance, quarters):
                act.wait_ge(x_updated, quarters) if quarters else act.wait_ge(x_loaded, 16)
                if instance:
                    act.wait_ge(rms_ready, instance)
                if instance == 1:
                    act.wait_ge(mem_squared, TT)
                for tt in range(TT):
                    if instance or tt:
                        act.wait_ge(x_squared, TT * instance + tt)
                    act.activation(squares[:, :], x_rows[:, tt, :], ACT.Square,
                                   accum_out=rms[:, 0, tt:tt + 1]).then_inc(x_squared, 1)

            def turn(first, pairs, layer=0, which=None):
                for p in range(pairs):
                    act.wait_ge(cols_turned, first + p + 1)
                    b = bank[4 + (p % 4)]
                    if which is None:
                        act.activation(c_hi[:, 2 * p:2 * p + 2, :], b[:, :].rearrange("p (k n) -> p k n", k=2),
                                       ACT.Copy).then_inc(cols_rounded, 1)
                    else:
                        act.activation(c_hi[:, 2 * p, :], b[:, 0:256], ACT.Copy, scale=gain_col(layer, which, 2 * p))
                        act.activation(c_hi[:, 2 * p + 1, :], b[:, 256:512], ACT.Copy,
                                       scale=gain_col(layer, which, 2 * p + 1)).then_inc(cols_rounded, 1)

            def ffn(f):
                base = ffn_piece(f)
                act.wait_ge(rms_spread, f + 1)
                act.activation(rms_cols[:, :], bank[6][:, 0:SEQ], ACT.Copy).then_inc(rms_cols_ready, 1)

                def silu(s, i=0):
                    act.wait_ge(gates_scaled, s + 1 + i)
                    act.activation(gate[:, :], gate[:, :], ACT.Silu).then_inc(gates_active, 1)

                def round_hidden(s, i=0, used=None):
                    act.wait_ge(hidden_ready, s + 1 + i)
                    if used is not None:
                        act.wait_ge(pieces_used, used + RING * i)
                    act.activation(h_hi[:, :], hidden[:, :], ACT.Copy).then_inc(hidden_rounded, 1)

                s0 = f * STEPS
                ahead(base, 2)
                silu(s0)
                ahead(base + 2, 2)
                round_hidden(s0)
                with act.Fori(0, STEPS - 2) as i:
                    n = base + 4
                    ahead(n, 2, i)
                    silu(s0 + 1, i)
                    ahead(n + 2, 4, i)
                    round_hidden(s0 + 1, i, n + 6)
                n = base + 4 + 6 * (STEPS - 2)
                ahead(n, 2)
                silu(s0 + STEPS - 1)
                ahead(n + 2, 4)
                round_hidden(s0 + STEPS - 1, 0, n + 6)
                ahead(n + 6, 2)

            def mem_part(layer):
                if layer:
                    act.wait_ge(pieces_used, (layer - 1) * P_LAYER + P_KV + 4)
                for kc in range(KC):
                    act.activation(m_hi[:, kc, :], mem_cols[:, kc, :], ACT.Copy,
                                   scale=gain_col(layer, 3, kc)).then_inc(mem_rounded, 1)

            def attend(events, layer):
                n0 = layer * P_LAYER
                for what, arg, n in events:
                    if what == "block":
                        b = arg
                        used = n0 + P_IN + 4 * b
                        ahead(used, 4)
                        if b == 0:
                            act.wait_ge(rms_ready, 4 * layer + 2)
                        act.wait_ge(pieces_used, used + 4)
                        act.activation(qkv[:, 0, b * HALF:(b + 1) * HALF], bank[(2 * b) % 4][:, :], ACT.Copy,
                                       scale=rms[:, 3, 0:1]).then_inc(rows0_stored, 1)
                    elif what == "turn_qk":
                        act.wait_ge(qk_turned, n["qk"] + 1)
                        act.activation(qk_cols[:, 2 * arg:2 * arg + 2, :],
                                       bank[4 + n["qk"] % 2][:, :].rearrange("p (k n) -> p k n", k=2),
                                       ACT.Copy).then_inc(qk_stored, 1)
                    elif what == "mem_kv":
                        ahead(n0 + P_KV, 2)
                        act.wait_ge(pieces_used, n0 + P_KV + 2)
                        act.activation(mem_k[:, :, :], bank[0][:, :].rearrange("p (k n) -> p k n", k=2),
                                       ACT.Copy).then_inc(mem_k_stored, 1)
                        ahead(n0 + P_KV + 2, 2)
                    elif what == "scores":
                        for j in range(len(arg.maps)):
                            m = n["map"] + j
                            wide = (128, 256) if arg.group != "m" else (256, 256)
                            act.wait_ge(masked, m + 1)
                            at = 0
                            for tt in range(TT):
                                view = probs[:, m % PLACES, at:at + wide[tt]]
                                total = sums[:, n["batch"] % 2, tt, arg.slot, j:j + 1]
                                if tt == 0 and j == 0 and arg.slot == 0 and n["batch"] >= 2:
                                    act.wait_ge(mixed_stored, n["batch"] - 1)
                                last = act.activation(view, view, ACT.Exp, scale=-1.0,
                                                      bias=bias[:, m % PLACES, tt:tt + 1], accum_out=total)
                                at += wide[tt]
                            last.then_inc(exped, 1)

            prepare(0)
            act.wait_ge(params_loaded, 16 * N_PARAMS)
            act.wait_ge(angles_ready, 1)
            act.activation(angle[:, 3, :, :, :], angle[:, 3, :, :, :], ACT.Sin).then_inc(sines_ready, 1)
            act.wait_ge(lambdas_summed, 1)
            act.activation(lam[:, 1, :, :], lam[:, 0, :, :], ACT.Exp).then_inc(lambdas_exp, 1)
            act.wait_ge(gains_turned, 1)
            act.activation(gains[:, :], bank[0][:, 0:10 * KC], ACT.Copy).then_inc(gains_ready, 1)
            for n in range(1, RING):
                prepare(n)
            act.wait_ge(gains_ready, 1)
            turn(0, 4, 0, 0)
            square(0, 0)
            act.wait_ge(mem_loaded, 16)
            act.wait_ge(x_squared, TT)
            for tt in range(TT):
                if tt:
                    act.wait_ge(mem_squared, tt)
                act.activation(squares[:, :], mixed[:, tt, :], ACT.Square,
                               accum_out=rms_a[:, 0, tt:tt + 1]).then_inc(mem_squared, 1)
            for p in range(4):
                act.wait_ge(mem_turned, p + 1)
                act.activation(mem_cols[:, 2 * p:2 * p + 2, :], bank[p][:, :].rearrange("p (k n) -> p k n", k=2),
                               ACT.Copy).then_inc(mem_cols_ready, 1)
            act.wait_ge(mem_cols_ready, 4)

            for layer in range(DEPTH):
                t0, x0 = layer * T_LAYER, layer * X_LAYER
                if layer:
                    turn(t0 + T_FFN1, 4, layer, 0)
                    square(4 * layer, x0)
                ffn(2 * layer)
                turn(t0 + T_MIX, 4, layer, 1)
                square(4 * layer + 1, x0 + X_FFN1 + 4)
                mem_part(layer)
                attend(layers[layer][0], layer)
                turn(t0 + T_OUT, 4)
                ahead(layer * P_LAYER + P_OUT, 8)
                turn(t0 + T_MQ, 4, layer, 2)
                square(4 * layer + 2, x0 + X_OUT + 4)
                ahead(layer * P_LAYER + P_MQ, 2)
                act.wait_ge(pieces_used, layer * P_LAYER + P_MQ + 2)
                act.activation(mem_q[:, :, :], bank[0][:, :].rearrange("p (k n) -> p k n", k=2),
                               ACT.Copy).then_inc(mem_q_stored, 1)
                attend(layers[layer][1], layer)
                turn(t0 + T_MO, 1)
                ahead(layer * P_LAYER + P_MO, 2)
                turn(t0 + T_FFN2, 4, layer, 4)
                square(4 * layer + 3, x0 + X_MO + 4)
                ffn(2 * layer + 1)
            square(4 * DEPTH, X_LAYER * DEPTH)

        @block.vector
        def _(dve):
            count = [0]

            def link(ins):
                count[0] += 1
                ins.then_inc(vector_done, 1)
                dve.wait_ge(vector_done, count[0])

            def prepare(n, i=0):
                if isinstance(n, int) and n >= PIECES:
                    return
                slot = n % RING
                dve.wait_ge(pieces_rounded, n + 1 + RING * i)
                dve.tensor_tensor(w_lo[:, slot, :], w_raw[:, n % RAW, :], raw(w_hi[:, slot, :]),
                                  ALU.subtract).then_inc(pieces_split, 1)

            def ahead(n, count=1, i=0):
                for k in range(count):
                    prepare(n + k + RING, i)

            def rsqrt(y, total, tmp, width, final):
                link(dve.tensor_scalar(total, total, 1.0 / width, EPS, ALU.mult, ALU.add))
                link(dve.tensor_scalar(y.bitcast(I32), total.bitcast(I32), -0.5, float(0x5F3759DF),
                                       ALU.mult, ALU.add))
                for k in range(3):
                    link(dve.scalar_tensor_tensor(tmp, y, -0.5, y, ALU.mult, ALU.mult))
                    link(dve.tensor_tensor(tmp, tmp, total, ALU.mult))
                    last = dve.scalar_tensor_tensor(y, tmp, 1.5, y, ALU.add, ALU.mult)
                    if k < 2 or final is None:
                        link(last)
                    else:
                        last.then_inc(final, 1)

            def norm(instance):
                dve.wait_ge(x_squared, TT * (instance + 1))
                rsqrt(rms[:, 3, :], rms[:, 0, :], rms[:, 2, :], D, rms_ready)
                dve.wait_ge(rms_ready, instance + 1)

            def spread(f):
                dve.tensor_scalar(diag[:, 0, :], ident, rms[:, 3, 0:1], None, ALU.mult)
                dve.tensor_scalar(diag[:, 1, :], ident, rms[:, 3, 1:2], None, ALU.mult).then_inc(diag_ready, 1)
                link(dve.tensor_scalar(rms_scaled[:, :], rms[:, 3, :], 0.5, None, ALU.mult))

            def turn(first, pairs, layer=0, which=None):
                for p in range(pairs):
                    dve.wait_ge(cols_rounded, first + p + 1)
                    b = bank[4 + (p % 4)]
                    hi, lo = c_hi[:, 2 * p:2 * p + 2, :], c_lo[:, 2 * p:2 * p + 2, :]
                    if which is None:
                        dve.tensor_tensor(lo, b[:, :].rearrange("p (k n) -> p k n", k=2), raw(hi),
                                          ALU.subtract).then_inc(cols_split, 1)
                    else:
                        for k in range(2):
                            last = dve.scalar_tensor_tensor(lo[:, k, :], b[:, k * 256:(k + 1) * 256],
                                                            gain_col(layer, which, 2 * p + k), raw(hi[:, k, :]),
                                                            ALU.mult, ALU.subtract)
                        last.then_inc(cols_split, 1)

            def update(used, scaled):
                dve.wait_ge(pieces_used, used)
                for dh in range(2):
                    for tt in range(TT):
                        x = x_rows[:, tt, dh * HALF:(dh + 1) * HALF]
                        b = bank[2 * tt + dh][:, :]
                        if scaled:
                            last = dve.scalar_tensor_tensor(x, b, rms_scaled[:, tt:tt + 1], x, ALU.mult, ALU.add)
                        else:
                            last = dve.tensor_tensor(x, b, x, ALU.add)
                        last.then_inc(x_updated, 1)

            def ffn(f):
                base = ffn_piece(f)
                s0 = f * STEPS

                def scale_gate(s, used, i=0):
                    dve.wait_ge(pieces_used, used + RING * i)
                    dve.tensor_tensor(gate[:, :].rearrange("p (c n) -> p c n", c=2),
                                      bank[GATE][:, :].rearrange("p (c n) -> p c n", c=2),
                                      rms_cols[:, :].unsqueeze(1).broadcast_to([P, 2, SEQ]),
                                      ALU.mult).then_inc(gates_scaled, 1)

                def multiply(s, used, i=0):
                    dve.wait_ge(pieces_used, used + RING * i)
                    dve.wait_ge(gates_active, s + 1 + i)
                    dve.tensor_tensor(hidden[:, :], bank[UP][:, :], gate[:, :], ALU.mult).then_inc(hidden_ready, 1)

                def split_hidden(s, i=0):
                    dve.wait_ge(hidden_rounded, s + 1 + i)
                    dve.tensor_tensor(h_lo[:, :], hidden[:, :], raw(h_hi[:, :]),
                                      ALU.subtract).then_inc(hidden_split, 1)

                dve.wait_ge(rms_cols_ready, f + 1)
                scale_gate(s0, base + 2)
                ahead(base, 2)
                multiply(s0, base + 4)
                ahead(base + 2, 2)
                split_hidden(s0)
                with dve.Fori(0, STEPS - 2) as i:
                    n = base + 4
                    scale_gate(s0 + 1, n + 2, i)
                    ahead(n, 3, i)
                    multiply(s0 + 1, n + 4, i)
                    ahead(n + 3, 3, i)
                    split_hidden(s0 + 1, i)
                n = base + 4 + 6 * (STEPS - 2)
                scale_gate(s0 + STEPS - 1, n + 2)
                ahead(n, 3)
                multiply(s0 + STEPS - 1, n + 4)
                ahead(n + 3, 3)
                split_hidden(s0 + STEPS - 1)
                ahead(n + 6, 2)
                update(n + 8, True)

            def mem_part(layer):
                for kc in range(KC):
                    dve.wait_ge(mem_rounded, layer * KC + kc + 1)
                    dve.scalar_tensor_tensor(m_lo[:, kc, :], mem_cols[:, kc, :], gain_col(layer, 3, kc),
                                             raw(m_hi[:, kc, :]), ALU.mult, ALU.subtract).then_inc(mem_split, 1)

            def finish_a(layer, n):
                b = bank[7][:, :].rearrange("p (t h d) -> p t h d", t=TT, h=A_HEADS)
                link(dve.tensor_copy(out_a[:, :, :, :], b))
                link(dve.tensor_tensor(sq_a[:, :, :, :], out_a[:, :, :, :], out_a[:, :, :, :], ALU.mult))
                link(dve.tensor_reduce(rms_a[:, 0, :], sq_a[:, :, :, :].rearrange("p t h d -> p (t h) d"),
                                       AX.X, ALU.add))
                rsqrt(rms_a[:, 3, :], rms_a[:, 0, :], rms_a[:, 2, :], HD, None)
                flat = out_a[:, :, :, :].rearrange("p t h d -> p (t h) d")
                factor = rms_a[:, 3, :].unsqueeze(2).broadcast_to([P, TT * A_HEADS, HD])
                link(dve.tensor_tensor(flat, flat, factor, ALU.mult))
                g = subln[:, layer, :].unsqueeze(1).broadcast_to([P, A_HEADS, HD])
                for tt in range(TT):
                    last = dve.tensor_tensor(mixed[:, tt, 0:A_HEADS * HD].rearrange("p (h d) -> p h d", d=HD),
                                             out_a[:, tt, :, :], g, ALU.mult)
                last.then_inc(mixed_stored, 1)

            def attend(events, layer):
                n0 = layer * P_LAYER
                for what, arg, n in events:
                    if what == "block":
                        b = arg
                        used = n0 + P_IN + 4 * b
                        ahead(used, 4)
                        dve.wait_ge(pieces_used, used + 4)
                        dve.tensor_scalar(qkv[:, 1, b * HALF:(b + 1) * HALF], bank[(2 * b + 1) % 4][:, :],
                                          rms[:, 3, 1:2], None, ALU.mult).then_inc(rows1_stored, 1)
                    elif what == "mem_kv":
                        ahead(n0 + P_KV, 4)
                        dve.wait_ge(pieces_used, n0 + P_KV + 4)
                        dve.tensor_copy(mem_v[:, :, :], bank[1][:, :].rearrange("p (k n) -> p k n", k=2))\
                           .then_inc(mem_v_stored, 1)
                    elif what == "scores":
                        for j in range(len(arg.maps)):
                            m = n["map"] + j
                            dve.wait_ge(scored, m + 1)
                            if m >= PLACES:
                                dve.wait_ge(probs_turned, place_free[m])
                            wide = (128, 256) if arg.group != "m" else (256, 256)
                            at = 0
                            for tt in range(TT):
                                if arg.group == "m":
                                    mask, scale = const[:, K_ZERO:K_ZERO + 256], rms_scaled[:, tt:tt + 1]
                                else:
                                    mask = const[:, arg.mask + at:arg.mask + at + wide[tt]]
                                    scale = -(len(arg.maps) / HD) ** 0.5
                                last = dve.tensor_tensor_reduce(
                                    probs[:, m % PLACES, at:at + wide[tt]], bank[4 + m % 2][:, at:at + wide[tt]], mask,
                                    scale, BIG, ALU.add, ALU.min, bias[:, m % PLACES, tt:tt + 1])
                                at += wide[tt]
                            last.then_inc(masked, 1)
                    elif what == "turn":
                        h = n["head"]
                        if arg.group == "a":
                            combine(arg, n, layer)
                        dve.wait_ge(probs_turned, h + 1)
                        if h >= 2:
                            dve.wait_ge(applied, h - 1)
                        wide = 384 if arg.group != "m" else 512
                        dve.tensor_copy(probs_t[:, h % 2, 0:wide], bank[6][:, 0:wide]).then_inc(probs_stored, 1)
                    elif what == "apply" and arg.last:
                        dve.wait_ge(applied, n["head"] + 1)
                        if arg.group == "a":
                            finish_a(layer, n)
                            continue
                        nh, half = arg.batch, n["batch"] % 2
                        dve.wait_ge(exped, n["map"] + 1)
                        link(dve.reciprocal(recips[:, half, :, 0:nh, 0], sums[:, half, :, 0:nh, 0]))
                        first = {"b": 256, "c": 640, "m": 0}[arg.group] + (arg.h - nh + 1) * HD
                        for tt in range(TT):
                            last = dve.tensor_tensor(
                                mixed[:, tt, first:first + nh * HD].rearrange("p (h d) -> p h d", d=HD),
                                bank[7][:, tt * nh * HD:(tt + 1) * nh * HD].rearrange("p (h d) -> p h d", d=HD),
                                recips[:, half, tt, 0:nh, 0].unsqueeze(2).broadcast_to([P, nh, HD]), ALU.mult)
                        last.then_inc(mixed_stored, 1)

            def combine(arg, n, layer):
                m, half, s = n["map"], n["batch"] % 2, arg.slot
                dve.wait_ge(exped, m + 2)
                link(dve.reciprocal(recips[:, half, :, s, :], sums[:, half, :, s, :]))
                link(dve.tensor_scalar(recips[:, half, :, s, 1], recips[:, half, :, s, 1], lam[:, 3, layer, 0:1],
                                       None, ALU.mult))
                for tt, (a, b) in enumerate(((0, 128), (128, 384))):
                    p1, p2 = probs[:, m % PLACES, a:b], probs[:, (m + 1) % PLACES, a:b]
                    link(dve.tensor_scalar(p2, p2, recips[:, half, tt, s, 1:2], None, ALU.mult))
                    last = dve.scalar_tensor_tensor(p1, p1, recips[:, half, tt, s, 0:1], p2, ALU.mult, ALU.add)
                last.then_inc(combined, 1)

            dve.wait_ge(params_loaded, 16 * N_PARAMS)
            link(dve.tensor_copy(pos_f[:, :], pos[:, :]))
            freq = const[:, K_FREQ:K_FREQ + NF]
            for tt in range(TT):
                for part in range(2):
                    last = dve.tensor_scalar(angle[:, 0, part, tt, :], freq, pos_f[:, tt:tt + 1], None, ALU.mult)
            link(last)
            magic = 1.5 * 2.0 ** 23
            for part in range(2):
                link(dve.tensor_scalar(angle[:, 1, part, :, :], angle[:, 0, part, :, :], 1 / (2 * math.pi),
                                       0.25 * part, ALU.mult, ALU.add))
            link(dve.tensor_scalar(angle[:, 1, :, :, :], angle[:, 1, :, :, :], magic, None, ALU.add))
            link(dve.tensor_scalar(angle[:, 1, :, :, :], angle[:, 1, :, :, :], -magic, None, ALU.add))
            c1 = 6.28125
            c2 = float(np.float32(round((2 * math.pi - c1) * 2 ** 20) / 2 ** 20))
            c3 = 2 * math.pi - c1 - c2
            source = angle[:, 0, :, :, :]
            for c in (c1, c2, c3):
                link(dve.scalar_tensor_tensor(angle[:, 3, :, :, :].rearrange("p a t f -> p (a t f)"),
                                              angle[:, 1, :, :, :].rearrange("p a t f -> p (a t f)"), -c,
                                              source.rearrange("p a t f -> p (a t f)"), ALU.mult, ALU.add))
                source = angle[:, 3, :, :, :]
            link(dve.tensor_scalar(angle[:, 3, 1, :, :], angle[:, 3, 1, :, :], math.pi / 2, None, ALU.add))
            dve.tensor_scalar(angle[:, 3, :, :, :], angle[:, 3, :, :, :], 3.1415925, -3.1415925,
                              ALU.min, ALU.max).then_inc(angles_ready, 1)
            for j in range(2):
                link(dve.tensor_tensor(lambdas[:, 2 * j, :, :], lambdas[:, 2 * j, :, :], lambdas[:, 2 * j + 1, :, :],
                                       ALU.mult))
                last = dve.tensor_reduce(lam[:, 0, j, :], lambdas[:, 2 * j, :, :], AX.X, ALU.add)
                if j == 0:
                    link(last)
            last.then_inc(lambdas_summed, 1)
            for layer in range(DEPTH):
                init = 0.8 - 0.6 * math.exp(-0.3 * layer)
                link(dve.tensor_scalar(subln[:, layer, :], subln[:, layer, :], 1.0 - init, None, ALU.mult))
            dve.wait_ge(lambdas_exp, 1)
            for layer in range(DEPTH):
                init = 0.8 - 0.6 * math.exp(-0.3 * layer)
                link(dve.tensor_tensor(lam[:, 2, layer, 0:1], lam[:, 1, 1, layer:layer + 1],
                                       lam[:, 1, 0, layer:layer + 1], ALU.subtract))
                link(dve.tensor_scalar(lam[:, 3, layer, 0:1], lam[:, 2, layer, 0:1], -init, None, ALU.add))
            dve.wait_ge(sines_ready, 1)
            for part, (head, small) in enumerate(((sin_h, sin_a), (cos_h, cos_a))):
                for table, at, n in ((head, 0, ROT // 2), (small, ROT // 2, ROT_A // 2)):
                    value = angle[:, 3, part, :, at:at + n]
                    dve.tensor_scalar(table[:, :, 0:n], value, 1.0 if part else -1.0, None, ALU.mult)
                    last = dve.tensor_copy(table[:, :, n:2 * n], value)
            last.then_inc(tables_ready, 1)
            for n in range(RING):
                prepare(n)
            dve.wait_ge(gains_ready, 1)
            turn(0, 4, 0, 0)
            norm(0)
            spread(0)
            dve.wait_ge(mem_squared, TT)
            rsqrt(rms_a[:, 3, 0:TT], rms_a[:, 0, 0:TT], rms_a[:, 2, 0:TT], D, None)
            for tt in range(TT):
                last = dve.tensor_scalar(mixed[:, tt, :], mixed[:, tt, :], rms_a[:, 3, tt:tt + 1], None, ALU.mult)
            last.then_inc(mem_scaled, 1)
            dve.wait_ge(mem_cols_ready, 4)

            for layer in range(DEPTH):
                t0 = layer * T_LAYER
                if layer:
                    turn(t0 + T_FFN1, 4, layer, 0)
                    norm(4 * layer)
                    spread(2 * layer)
                ffn(2 * layer)
                turn(t0 + T_MIX, 4, layer, 1)
                norm(4 * layer + 1)
                mem_part(layer)
                attend(layers[layer][0], layer)
                turn(t0 + T_OUT, 4)
                ahead(layer * P_LAYER + P_OUT, 8)
                update(layer * P_LAYER + P_OUT + 8, False)
                turn(t0 + T_MQ, 4, layer, 2)
                norm(4 * layer + 2)
                link(dve.tensor_scalar(rms_scaled[:, :], rms[:, 3, :], -HD ** -0.5, None, ALU.mult))
                ahead(layer * P_LAYER + P_MQ, 2)
                attend(layers[layer][1], layer)
                turn(t0 + T_MO, 1)
                ahead(layer * P_LAYER + P_MO, 2)
                update(layer * P_LAYER + P_MO + 2, False)
                turn(t0 + T_FFN2, 4, layer, 4)
                norm(4 * layer + 3)
                spread(2 * layer + 1)
                ffn(2 * layer + 1)
            norm(4 * DEPTH)
            dve.wait_ge(final_loaded, 16)
            for tt in range(TT):
                dve.scalar_tensor_tensor(x_rows[:, tt, :], x_rows[:, tt, :], rms[:, 3, tt:tt + 1],
                                         final_gain, ALU.mult, ALU.mult).then_inc(out_ready, 1)

        @block.tensor
        def _(pe):
            reader = {}

            def claim(b):
                if b in reader:
                    pe.wait_ge(*reader[b])

            def three(out_, lhs, rhs, start, stop):
                (lh, ll), (rh, rl) = lhs, rhs
                pe.matmul(out_, lh, rh, start=start, stop=False, skip_group_check=True)
                pe.matmul(out_, ll, rh, start=False, stop=False, skip_group_check=True)
                return pe.matmul(out_, lh, rl, start=False, stop=stop, skip_group_check=True)

            def w(slot, a, b):
                return w_hi[:, slot, a:b], w_lo[:, slot, a:b]

            def col(kc, a, b):
                return c_hi[:, kc, a:b], c_lo[:, kc, a:b]

            def turn(first, pairs, source, ready):
                for p in range(pairs):
                    b = 4 + p % 4
                    if ready(p) is not None:
                        pe.wait_ge(*ready(p))
                    claim(b)
                    for k in range(2):
                        for tt in range(TT):
                            at = k * 256 + tt * P
                            last = pe.transpose(bank[b][:, at:at + P],
                                                source[:, tt, (2 * p + k) * P:(2 * p + k + 1) * P], ident)
                    last.then_inc(cols_turned, 1)
                    reader[b] = (cols_split, first + p + 1)

            def ffn(f, cols_at):
                base = ffn_piece(f)
                s0 = f * STEPS

                def columns(n, b, i=0, wait_cols=False):
                    for half in range(2):
                        slot = (n + half) % RING
                        pe.wait_ge(pieces_split, n + half + 1 + RING * i)
                        for k in range(4):
                            kc = 4 * half + k
                            if wait_cols and k % 2 == 0:
                                pe.wait_ge(cols_split, cols_at + kc // 2 + 1)
                            for fc in range(2):
                                at = k * 256 + fc * P
                                last = three(bank[b][:, fc * 256:(fc + 1) * 256], w(slot, at, at + P),
                                             col(kc, 0, SEQ), start=(kc == 0 and fc == 0),
                                             stop=(kc == KC - 1))
                        last.then_inc(pieces_used, 1)

                def down(n, s, first, final, i=0):
                    pe.wait_ge(hidden_split, s + 1 + i)
                    if first:
                        for b in range(4):
                            claim(b)
                    for half in range(2):
                        slot = (n + half) % RING
                        pe.wait_ge(pieces_split, n + half + 1 + RING * i)
                        for dh in range(2):
                            for tt in range(TT):
                                at = half * 256 + tt * P
                                last = three(bank[2 * tt + dh][:, :], (h_hi[:, at:at + P], h_lo[:, at:at + P]),
                                             w(slot, dh * HALF, (dh + 1) * HALF),
                                             start=first and half == 0, stop=final and half == 1)
                        last.then_inc(pieces_used, 1)

                claim(GATE)
                columns(base, GATE, wait_cols=True)
                pe.wait_ge(diag_ready, f + 1)
                claim(6)
                for tt in range(TT):
                    last = pe.matmul(bank[6][:, tt * P:(tt + 1) * P], const[:, K_ONE:K_ONE + P], diag[:, tt, :],
                                     start=True, stop=True)
                last.then_inc(rms_spread, 1)
                reader[6] = (rms_cols_ready, f + 1)
                claim(UP)
                columns(base + 2, UP)
                pe.wait_ge(gates_scaled, s0 + 1)
                columns(base + 4, GATE)
                pe.wait_ge(hidden_ready, s0 + 1)
                columns(base + 6, UP)
                down(base + 8, s0, True, False)
                with pe.Fori(0, STEPS - 2) as i:
                    n = base + 10
                    pe.wait_ge(gates_scaled, s0 + 2 + i)
                    columns(n, GATE, i)
                    pe.wait_ge(hidden_ready, s0 + 2 + i)
                    columns(n + 2, UP, i)
                    down(n + 4, s0 + 1, False, False, i)
                down(base + P_FFN - 2, s0 + STEPS - 1, False, True)
                reader[GATE] = (gates_scaled, s0 + STEPS)
                reader[UP] = (hidden_ready, s0 + STEPS)

            def rows_product(n, ks, ready, x_end):
                for b in range(4):
                    claim(b)
                for kc in range(ks):
                    slot = (n + kc) % RING
                    pe.wait_ge(pieces_split, n + kc + 1)
                    if kc % 2 == 0:
                        pe.wait_ge(cols_split, ready + kc // 2 + 1)
                    for dh in range(2):
                        for tt in range(TT):
                            last = three(bank[2 * tt + dh][:, :], col(kc, tt * P, (tt + 1) * P),
                                         w(slot, dh * HALF, (dh + 1) * HALF), start=kc == 0, stop=kc == ks - 1)
                    last.then_inc(pieces_used, 1)
                for b in range(4):
                    reader[b] = (x_updated, x_end)

            def cols_product(n, b, cols, ready):
                claim(b)
                for half in range(2):
                    slot = (n + half) % RING
                    pe.wait_ge(pieces_split, n + half + 1)
                    for k in range(4):
                        kc = 4 * half + k
                        pe.wait_ge(*ready(kc))
                        for fc in range(2):
                            at = k * 256 + fc * P
                            last = three(bank[b][:, fc * 256:(fc + 1) * 256], w(slot, at, at + P), cols(kc),
                                         start=(kc == 0 and fc == 0), stop=(kc == KC - 1))
                    last.then_inc(pieces_used, 1)

            def attend(events, layer):
                n0 = layer * P_LAYER
                for what, arg, n in events:
                    if what == "block":
                        b = arg
                        for tt in range(TT):
                            claim((2 * b + tt) % 4)
                        for j in range(4):
                            piece = n0 + P_IN + 4 * b + j
                            pe.wait_ge(pieces_split, piece + 1)
                            if b == 0:
                                pe.wait_ge(cols_split, layer * T_LAYER + T_MIX + j + 1)
                            for k in range(2):
                                for tt in range(TT):
                                    last = three(bank[(2 * b + tt) % 4][:, :], col(2 * j + k, tt * P, (tt + 1) * P),
                                                 w(piece % RING, k * HALF, (k + 1) * HALF),
                                                 start=(j == 0 and k == 0), stop=(j == 3 and k == 1))
                            last.then_inc(pieces_used, 1)
                        reader[(2 * b) % 4] = (rows0_stored, layer * BLOCKS + b + 1)
                        reader[(2 * b + 1) % 4] = (rows1_stored, layer * BLOCKS + b + 1)
                    elif what == "turn_qk":
                        pe.wait_ge(rotated, layer * 3 + {0: 1, 1: 1, 2: 2, 3: 2, 4: 2}.get(arg, 3))
                        b = 4 + n["qk"] % 2
                        claim(b)
                        for k in range(2):
                            blk = 2 * arg + k
                            first = blk * P if blk < 4 else (BQ + (blk - 4) * P if blk < 10 else CQ + (blk - 10) * P)
                            for tt in range(TT):
                                at = k * 256 + tt * P
                                last = pe.transpose(bank[b][:, at:at + P], qkv[:, tt, first:first + P], ident)
                        last.then_inc(qk_turned, 1)
                        reader[b] = (qk_stored, n["qk"] + 1)
                    elif what == "mem_kv":
                        piece = n0 + P_KV
                        cols_product(piece, 0, lambda kc: (m_hi[:, kc, :], m_lo[:, kc, :]),
                                     lambda kc: (mem_split, layer * KC + kc + 1))
                        reader[0] = (mem_k_stored, layer + 1)
                        claim(1)
                        for half in range(2):
                            slot = (piece + 2 + half) % RING
                            pe.wait_ge(pieces_split, piece + 2 + half + 1)
                            for k in range(4):
                                kc = 4 * half + k
                                for tt in range(TT):
                                    last = three(bank[1][:, tt * 256:(tt + 1) * 256],
                                                 (m_hi[:, kc, tt * P:(tt + 1) * P], m_lo[:, kc, tt * P:(tt + 1) * P]),
                                                 w(slot, k * 256, (k + 1) * 256),
                                                 start=(kc == 0 and tt == 0), stop=(kc == KC - 1))
                            last.then_inc(pieces_used, 1)
                        reader[1] = (mem_v_stored, layer + 1)
                    elif what == "scores":
                        mem = arg.group == "m"
                        if mem and arg.h == 0:
                            pe.wait_ge(mem_q_stored, layer + 1)
                            pe.wait_ge(mem_k_stored, layer + 1)
                        elif arg.h == 0:
                            pe.wait_ge(qk_stored, layer * 8 + {"a": 2, "b": 5, "c": 8}[arg.group])
                        for j, (qb, kb, p0, ps) in enumerate(arg.maps):
                            m = n["map"] + j
                            b = 4 + m % 2
                            claim(b)
                            at = 0
                            for tt in range(TT):
                                keys = 256 if mem else (tt + 1) * P
                                q, k = (mem_q, mem_k) if mem else (qk_cols, qk_cols)
                                last = pe.matmul(bank[b][:, at:at + keys], q[p0:p0 + ps, qb, tt * P:(tt + 1) * P],
                                                 k[p0:p0 + ps, kb, 0:keys], start=True, stop=True)
                                at += keys
                            last.then_inc(scored, 1)
                            reader[b] = (masked, m + 1)
                    elif what == "turn":
                        h, m = n["head"], n["map"]
                        if arg.group == "a":
                            pe.wait_ge(combined, layer * A_HEADS + arg.h + 1)
                        else:
                            pe.wait_ge(exped, m + 1)
                        claim(6)
                        for k in range(4 if arg.group == "m" else 3):
                            last = pe.transpose(bank[6][:, k * P:(k + 1) * P], probs[:, m % PLACES, k * P:(k + 1) * P], ident)
                        last.then_inc(probs_turned, 1)
                        reader[6] = (probs_stored, h + 1)
                    elif what == "apply":
                        h = n["head"]
                        pe.wait_ge(probs_stored, h + 1)
                        if arg.slot == 0:
                            claim(7)
                            if arg.group == "m":
                                pe.wait_ge(mem_v_stored, layer + 1)
                            else:
                                stored = layer * BLOCKS + {"a": 2, "b": 4, "c": 6}[arg.group]
                                pe.wait_ge(rows0_stored, stored)
                                pe.wait_ge(rows1_stored, stored)
                        for tt in range(TT):
                            at = (tt * arg.batch + arg.slot) * HD
                            if arg.group == "m":
                                terms = [(2 * tt, 0), (2 * tt + 1, 1)]
                            else:
                                terms = [(0, 0)] if tt == 0 else [(1, 0), (2, 1)]
                            for k, (blk, vt) in enumerate(terms):
                                v = mem_v if arg.group == "m" else qkv
                                last = pe.matmul(bank[7][:, at:at + HD], probs_t[:, h % 2, blk * P:(blk + 1) * P],
                                                 v[:, vt, arg.v_col:arg.v_col + HD],
                                                 start=k == 0, stop=k == len(terms) - 1)
                        last.then_inc(applied, 1)
                        if arg.last:
                            reader[7] = (mixed_stored, n["batch"] + 1)

            pe.wait_ge(params_loaded, 16 * N_PARAMS)
            pe.transpose(bank[0][:, 0:10 * KC], gain_rows[:, :], const[0:10 * KC, K_ID:K_ID + 10 * KC])\
              .then_inc(gains_turned, 1)
            reader[0] = (gains_ready, 1)
            turn(0, 4, x_rows, lambda p: (x_loaded, 16))
            pe.wait_ge(mem_scaled, 1)
            for p in range(4):
                claim(p)
                for k in range(2):
                    for tt in range(TT):
                        at = k * 256 + tt * P
                        last = pe.transpose(bank[p][:, at:at + P], mixed[:, tt, (2 * p + k) * P:(2 * p + k + 1) * P],
                                            ident)
                last.then_inc(mem_turned, 1)
                reader[p] = (mem_cols_ready, p + 1)

            for layer in range(DEPTH):
                t0, x0, n0 = layer * T_LAYER, layer * X_LAYER, layer * P_LAYER

                def updated(stage):
                    return lambda p: (x_updated, x0 + stage + (2 if p < 2 else 4))

                if layer:
                    turn(t0 + T_FFN1, 4, x_rows, updated(0 - 4))
                ffn(2 * layer, t0 + T_FFN1)
                for b in range(4):
                    reader[b] = (x_updated, x0 + X_FFN1 + 4)
                turn(t0 + T_MIX, 4, x_rows, updated(X_FFN1))
                attend(layers[layer][0], layer)
                turn(t0 + T_OUT, 4, mixed, lambda p: (mixed_stored, layer * 6 + 5))
                rows_product(n0 + P_OUT, 8, t0 + T_OUT, x0 + X_OUT + 4)
                turn(t0 + T_MQ, 4, x_rows, updated(X_OUT))
                cols_product(n0 + P_MQ, 0, lambda kc: col(kc, 0, SEQ),
                             lambda kc: (cols_split, t0 + T_MQ + kc // 2 + 1))
                reader[0] = (mem_q_stored, layer + 1)
                attend(layers[layer][1], layer)
                turn(t0 + T_MO, 1, mixed, lambda p: (mixed_stored, layer * 6 + 6))
                rows_product(n0 + P_MO, 2, t0 + T_MO, x0 + X_MO + 4)
                turn(t0 + T_FFN2, 4, x_rows, updated(X_MO))
                ffn(2 * layer + 1, t0 + T_FFN2)
                for b in range(4):
                    reader[b] = (x_updated, x0 + X_FFN2 + 4)


_INS = ["x", "mem", "positions", "ffn1_norm", "ffn1_w_gate", "ffn1_w_up", "ffn1_w_down", "mix_norm", "w_in", "w_out",
        "diff_lambda_q1", "diff_lambda_k1", "diff_lambda_q2", "diff_lambda_k2", "diff_subln", "memq_norm",
        "memkv_norm", "mem_w_q", "mem_w_kv", "mem_w_o", "ffn2_norm", "ffn2_w_gate", "ffn2_w_up", "ffn2_w_down",
        "final_norm"]


def kernel(**inputs):
    import concourse.bacc as bacc
    from concourse.bass_utils import run_bass_kernel_spmd

    nc = bacc.Bacc("TRN2", target_bir_lowering=False, num_devices=1)
    arrays, t = {}, {}

    def add(name, a):
        arrays[f"in_{name}_dram"] = a
        return nc.dram_tensor(f"in_{name}_dram", a.shape, mybir.dt.from_np(a.dtype), kind="ExternalInput").ap()

    for name in _INS:
        t[name] = add(name, np.ascontiguousarray(inputs[name]))
    constants = add("shape_constants", shape_constants())
    out = nc.dram_tensor("out_0_dram", (1, SEQ, D), F32, kind="ExternalOutput").ap()
    decoder_trunk(nc, t, constants, out)
    r = run_bass_kernel_spmd(nc, [arrays], core_ids=[0])
    return r.results[0]["out_0_dram"]
```

```python
import math
from contextlib import ExitStack

import numpy as np

import concourse.bass as bass
from concourse import mybir

F32 = mybir.dt.float32
F32R = mybir.dt.float32r
BF16 = mybir.dt.bfloat16
I32 = mybir.dt.int32
ALU = mybir.AluOpType
ACT = mybir.ActivationFunctionType
AX = mybir.AxisListType

P = 128
D = 1024
SEQ = 256
MEM = 256
DEPTH = 2
FF = 2816
HD = 64
A_HEADS, B_HEADS, C_HEADS = 4, 6, 6
A_MAP = HD // 2
MEM_HEADS = 4
EPS = 1e-6
NEG = -1e30
BIG = 3e38
ROPE_THETA = 500000.0
BRANCHES = ((128, 1), (512, 4), (2048, 16))

TT = SEQ // P
KC = D // P
PIECE = 1024
RING = 6
RAW = 3
STEPS = FF // 256
HALF = 512

AQ, AK, AV = 0, 256, 512
BQ, BK, BV = 768, 1152, 1536
CQ, CK, CV = 1920, 2304, 2688
BLOCKS = 3 * D // HALF
PLACES = 6

P_FFN = 6 * STEPS
P_MID = 40
P_FFN2 = P_FFN + P_MID
P_LAYER = P_FFN2 + P_FFN
PIECES = DEPTH * P_LAYER

STAGES = 4
LAST_STAGE = STAGES * DEPTH
MIXED_PAIRS = 5
BATCHES = 6
T_FFN1, T_MIX, T_OUT, T_MQ, T_MO, T_FFN2, T_LAYER = 0, 4, 8, 12, 16, 17, 21

ROT, ROT_A = HD // 4, A_MAP // 4
NF = ROT // 2 + ROT_A // 2

N_PARAMS = 1 + TT + 4 + 1
N_GAINS = 1 + 5

K_CAUSAL, K_DILATED, K_ZERO, K_ID, K_ONE, K_FREQ = 0, 384, 768, 1024, 1152, 1280
K_COLS = K_FREQ + NF


def shape_constants():
    out = np.zeros((P, K_COLS), np.float32)
    for tile, first, keys in ((0, 0, 128), (1, 128, 256)):
        delta = (tile * P + np.arange(P))[:, None] - np.arange(keys)[None, :]
        count = np.zeros(delta.shape)
        for window, dilation in BRANCHES:
            count += (delta >= 0) & (delta % dilation == 0) & (delta <= window)
        out[:, K_CAUSAL + first:K_CAUSAL + first + keys] = np.where(delta >= 0, 0.0, NEG)
        out[:, K_DILATED + first:K_DILATED + first + keys] = np.where(
            count > 0, math.sqrt(HD) * np.log(np.maximum(count, 1)), NEG)
    out[:, K_ID:K_ID + P] = np.eye(P)
    out[:, K_ONE:K_ONE + P] = 1.0
    theta = np.float32(ROPE_THETA)
    for at, rot in ((0, ROT), (ROT // 2, ROT_A)):
        out[:, K_FREQ + at:K_FREQ + at + rot // 2] = theta ** (-np.arange(0, rot, 2, dtype=np.float32) / np.float32(rot))
    return out


class Head:

    def __init__(self, group, h, maps, v_col, mask, batch, slot, last):
        self.group, self.h, self.maps, self.v_col, self.mask = group, h, maps, v_col, mask
        self.batch, self.slot, self.last = batch, slot, last


def heads_of(group):
    out = []
    if group == "a":
        for h in range(A_HEADS):
            maps = [((2 * h + j) // 4, 2 + (2 * h + j) // 4, 32 * ((2 * h + j) % 4), 32) for j in (0, 1)]
            out.append(Head(group, h, maps, AV + h * HD, K_CAUSAL, 4, h, h == 3))
    elif group in "bc":
        q0, k0, v0 = (4, 7, BV) if group == "b" else (10, 13, CV)
        mask = K_DILATED if group == "b" else K_CAUSAL
        for h in range(B_HEADS):
            out.append(Head(group, h, [(q0 + h // 2, k0 + h // 2, 64 * (h % 2), 64)],
                            v0 + h * HD, mask, 3, h % 3, h % 3 == 2))
    else:
        for h in range(MEM_HEADS):
            out.append(Head(group, h, [(h // 2, h // 2, 64 * (h % 2), 64)], h * HD, K_ZERO, 4, h, h == 3))
    return out


def middle_events(layer):
    def steps(group):
        heads = heads_of(group)
        for i in range(len(heads) + 3):
            out = []
            if i < len(heads):
                out.append(("scores", heads[i]))
            if 0 <= i - 2 < len(heads):
                out.append(("turn", heads[i - 2]))
            if 0 <= i - 3 < len(heads):
                out.append(("apply", heads[i - 3]))
            if group == "a" and 0 <= i - 1 < len(heads):
                out.append(("combine", heads[i - 1]))
            yield out

    a, b, c, m = (steps(g) for g in "abcm")
    ev = []

    def put(*parts):
        for x in parts:
            ev.extend(x if isinstance(x, list) else [x])

    def qk(*pairs):
        return [("turn_qk", p) for p in pairs]

    put(("in", (0, 0)))
    if layer == 0:
        put(("tables", 0), ("mem_norm", 0))
    put(("in", (0, 1)), ("norm", 1), ("in", (0, 2)), ("in", (0, 3)), ("in", (1, 0)), ("store_in", 0))
    if layer == 0:
        put([("turn_mem", p) for p in range(4)])
    for j in range(1, 4):
        put(("in", (1, j)), ("mem_gain", 2 * j - 2), ("mem_gain", 2 * j - 1))
    put(("in", (2, 0)), ("store_in", 1), ("rotate", "a"), ("mem_gain", 6), ("mem_gain", 7), ("in", (2, 1)), qk(0, 1),
        ("in", (2, 2)), next(a), ("in", (2, 3)), next(a), ("in", (3, 0)), ("store_in", 2), next(a))
    for j in range(1, 4):
        put(("in", (3, j)), next(a))
    put(("in", (4, 0)), ("store_in", 3), ("rotate", "b"), next(a), ("in", (4, 1)), qk(2, 3), ("in", (4, 2)), qk(4),
        ("in", (4, 3)), next(b), ("in", (5, 0)), ("store_in", 4), next(b))
    for j in range(1, 4):
        put(("in", (5, j)), next(b))
    put(("mem_k", 0), ("store_in", 5), ("rotate", "c"), next(b), ("turn_mixed", 0), ("mem_k", 1), next(b),
        ("out", 0), ("store_k", 0), next(b), qk(5, 6), ("out", 1), next(b), qk(7), next(c), ("turn_mixed", 1), next(c), ("out", 2),
        next(c), next(c), next(c), ("out", 3), next(c), ("turn_mixed", 2), next(c), ("out", 4), next(c), next(c),
        ("out", 5), ("turn_mixed", 3), ("out", 6), ("out", 7))
    put(("residual", 2), ("mem_v", 0), ("mem_q", 0), ("norm", 2), ("mem_q", 1), ("store_q", 0), next(m),
        ("mem_v", 1), next(m), ("store_v", 0))
    for x in m:
        put(x)
    put(("turn_mixed", 4), ("mem_o", 0), ("mem_o", 1))
    assert not list(a) + list(b) + list(c)
    return ev


PIECE_EVENTS = ("in", "out", "mem_k", "mem_v", "mem_q", "mem_o")


def number_events():
    count = {"head": 0, "map": 0, "batch": 0, "turn_qk": 0, "turn_mixed": 0}
    layers = []
    for layer in range(DEPTH):
        piece = layer * P_LAYER + P_FFN
        heads, part = {}, []
        events = middle_events(layer)
        for what, arg in events:
            if what == "scores":
                heads[arg.group, arg.h] = {k: count[k] for k in ("head", "map", "batch")}
                count["head"] += 1
                count["map"] += len(arg.maps)
                count["batch"] += arg.last
        for what, arg in events:
            n = {}
            if what in PIECE_EVENTS:
                n = {"piece": piece}
                piece += 1
            elif what in ("scores", "turn", "apply", "combine"):
                n = heads[arg.group, arg.h]
            elif what in count:
                n = {what: count[what]}
                count[what] += 1
            part.append((what, arg, n))
        assert piece == layer * P_LAYER + P_FFN2
        layers.append(part)
    return layers, count


def decoder_trunk(nc, t, constants, out):
    layers, count = number_events()
    with ExitStack() as ctx:
        def sb(name, shape, dt=F32):
            return ctx.enter_context(nc.sbuf_tensor(name, shape, dt))

        def sem(name):
            return ctx.enter_context(nc.semaphore(name))

        x_cols = sb("x_cols", [P, KC, SEQ])
        w_raw = sb("w_raw", [P, RAW, PIECE])
        w_hi = sb("w_hi", [P, RING, PIECE], F32R)
        w_lo = sb("w_lo", [P, RING, PIECE], F32R)
        c_hi = sb("c_hi", [P, KC, SEQ], F32R)
        c_lo = sb("c_lo", [P, KC, SEQ], F32R)
        mem_cols = sb("mem_cols", [P, KC, MEM])
        m_hi = sb("m_hi", [P, KC, MEM], F32R)
        m_lo = sb("m_lo", [P, KC, MEM], F32R)
        mem_k = sb("mem_k", [P, 2, MEM])
        mem_q = sb("mem_q", [P, 2, SEQ])
        mem_v = sb("mem_v", [P, TT, MEM_HEADS * HD])
        qkv = sb("qkv", [P, TT, 3 * D])
        qk_cols = sb("qk_cols", [P, 16, SEQ])
        mixed = sb("mixed", [P, TT, D])
        x_in = qkv[:, :, 0:D]
        mem_rows = qkv[:, :, 2 * D:3 * D]
        out_rows = qkv[:, :, 0:D]
        squares = mixed[:, :, :].rearrange("p t (k n) -> p (t k) n", n=SEQ)
        probs = sb("probs", [P, PLACES, HALF])
        probs_t = sb("probs_t", [P, 2, HALF])
        bias = sb("bias", [P, PLACES, TT])
        sums = sb("sums", [P, 2, TT, 4, 2])
        recips = sb("recips", [P, 2, TT, 4, 2])
        out_a = sb("out_a", [P, TT, A_HEADS, HD])
        sq_a = sb("sq_a", [P, TT, A_HEADS, HD])
        rms_a = sb("rms_a", [P, 4, TT * A_HEADS])
        rot_1 = sb("rot_1", [P, TT, 2 * B_HEADS * ROT])
        rot_2 = sb("rot_2", [P, TT, 2 * B_HEADS * ROT])
        gate = sb("gate", [P, HALF])
        hidden = sb("hidden", [P, HALF])
        h_hi = sb("h_hi", [P, HALF], F32R)
        h_lo = sb("h_lo", [P, HALF], F32R)
        last_hi, last_lo = (m[:, 0:2, :].rearrange("p k n -> p (k n)") for m in (m_hi, m_lo))
        rms = sb("rms", [P, 4, TT])
        rms_scaled = sb("rms_scaled", [P, TT])
        diag = sb("diag", [P, TT, P])
        rms_cols = sb("rms_cols", [P, SEQ])
        const = sb("const", [P, K_COLS])
        gain_rows = sb("gain_rows", [10 * KC, P])
        gains = sb("gains", [P, 10 * KC])
        final_gain = qk_cols[:, 0:D // SEQ, :].rearrange("p k n -> p (k n)")
        lambdas = sb("lambdas", [P, 4, DEPTH, A_MAP])
        lam = sb("lam", [P, 4, DEPTH, 2])
        subln = sb("subln", [P, DEPTH, HD])
        pos = sb("pos", [P, TT], I32)
        pos_f = sb("pos_f", [P, TT])
        angle = sb("angle", [P, 4, 2, TT, NF])
        cos_h = sb("cos_h", [P, TT, ROT])
        sin_h = sb("sin_h", [P, TT, ROT])
        cos_a = sb("cos_a", [P, TT, ROT_A])
        sin_a = sb("sin_a", [P, TT, ROT_A])

        ident = const[:, K_ID:K_ID + P]
        bank = [ctx.enter_context(nc.psum_tensor(f"bank{i}", [P, HALF], F32)) for i in range(8)]
        GATE, UP = 4, 5
        MEM_K, MEM_V, MEM_Q = 1, 7, 0
        OUT_BANKS = ((4, 5), (7, 0))

        params_loaded = sem("params_loaded")
        gains_loaded = sem("gains_loaded")
        x_loaded = [sem(f"x_loaded{i}") for i in range(2)]
        mem_loaded = sem("mem_loaded")
        weights_loaded = [sem(f"weights_loaded{i}") for i in range(RAW)]
        pieces_rounded = sem("pieces_rounded")
        pieces_split = sem("pieces_split")
        pieces_used = sem("pieces_used")
        vector_done = sem("vector_done")
        pool_done = sem("pool_done")
        gains_turned = sem("gains_turned")
        gains_ready = sem("gains_ready")
        lambdas_summed = sem("lambdas_summed")
        lambdas_exp = sem("lambdas_exp")
        angles_ready = sem("angles_ready")
        sines_ready = sem("sines_ready")
        tables_ready = sem("tables_ready")
        mem_squared = sem("mem_squared")
        mem_scaled = sem("mem_scaled")
        mem_turned = sem("mem_turned")
        mem_cols_ready = sem("mem_cols_ready")
        mem_rounded = sem("mem_rounded")
        mem_split = sem("mem_split")
        x_turned = sem("x_turned")
        quarter_done = sem("quarter_done")
        x_updated = sem("x_updated")
        squares_added = sem("squares_added")
        squares_summed = sem("squares_summed")
        x_squared = sem("x_squared")
        rms_ready = sem("rms_ready")
        diag_ready = sem("diag_ready")
        rms_spread = sem("rms_spread")
        rms_cols_ready = sem("rms_cols_ready")
        mixed_turned = sem("mixed_turned")
        cols_rounded = sem("cols_rounded")
        cols_split = sem("cols_split")
        gates_scaled = sem("gates_scaled")
        gates_active = sem("gates_active")
        gates_weighted = sem("gates_weighted")
        hidden_ready = sem("hidden_ready")
        hidden_rounded = sem("hidden_rounded")
        hidden_split = sem("hidden_split")
        rows0_stored = sem("rows0_stored")
        rows1_stored = sem("rows1_stored")
        rotated = sem("rotated")
        qk_turned = sem("qk_turned")
        qk_stored = sem("qk_stored")
        mem_k_stored = sem("mem_k_stored")
        mem_v_stored = sem("mem_v_stored")
        mem_q_stored = sem("mem_q_stored")
        scored = sem("scored")
        masked = sem("masked")
        exped = sem("exped")
        combined = sem("combined")
        probs_turned = sem("probs_turned")
        probs_stored = sem("probs_stored")
        applied = sem("applied")
        mixed_stored = sem("mixed_stored")
        final_loaded = sem("final_loaded")
        out_turned = sem("out_turned")
        out_ready = sem("out_ready")
        out_stored = sem("out_stored")

        def raw(view):
            return view.bitcast(F32)

        def gain_col(layer, which, kc):
            at = (which * DEPTH + layer) * KC + kc
            return gains[:, at:at + 1]

        def kind_of_ffn(f):
            return f // 2, f % 2

        def ffn_piece(f):
            layer, which = kind_of_ffn(f)
            return layer * P_LAYER + which * P_FFN2

        def stage_gain(stage, kc):
            return gain_col(stage // STAGES, (0, 1, 2, 4)[stage % STAGES], kc)

        def last_piece(layer, what, arg):
            return next(n["piece"] for w, a, n in layers[layer] if w == what and a == arg) + 1

        def end_piece(stage):
            layer, which = stage // STAGES, stage % STAGES
            if which == 2:
                return last_piece(layer, "out", KC - 1)
            return layer * P_LAYER + (0, P_FFN, None, P_FFN2)[which]

        def ready_quarter(stage, p):
            if stage == 0:
                return x_turned, p + 1
            if p < 3:
                return quarter_done, 3 * (stage - 1) + p + 1
            return pieces_used, end_piece(stage)

        owner = {n["map"] + j: n["head"] for part in layers for what, arg, n in part
                 if what == "scores" for j in range(len(arg.maps))}
        place_free = {m: owner[m - PLACES] + 1 for m in owner if m >= PLACES}
        n_heads = count["head"]

        block = ctx.enter_context(nc.Block())

        @block.sync
        def _(sp):
            def load_piece(n, i, source):
                slot = n % RAW
                if n >= RAW:
                    sp.wait_ge(pieces_split, n - RAW + 1 + RING * i)
                sp.dma_start(w_raw[:, slot, :].rearrange("p (k n) -> p k n", n=source.shape[-1]),
                             source).then_inc(weights_loaded[slot], 16)

            def up_source(w, half, i):
                view = w.rearrange("(h k p) f -> p h k f", h=2, p=P)
                return view[:, half, :, bass.ds(i * 256, 256)]

            def down_source(w, half, i):
                view = w.rearrange("(c h p) n -> p c h n", h=2, p=P)
                return view[:, bass.ds(i, 1), half, :]

            def load_ffn(f):
                layer, which = kind_of_ffn(f)
                name = "ffn1" if which == 0 else "ffn2"
                wg, wu, wd = (t[f"{name}_w_{x}"][layer] for x in ("gate", "up", "down"))
                base = ffn_piece(f)

                for j, source in enumerate((up_source(wg, 0, 0), up_source(wg, 1, 0),
                                            up_source(wu, 0, 0), up_source(wu, 1, 0))):
                    load_piece(base + j, 0, source)
                with sp.Fori(0, STEPS - 1) as i:
                    for j, source in enumerate((up_source(wg, 0, i + 1), up_source(wg, 1, i + 1),
                                                up_source(wu, 0, i + 1), up_source(wu, 1, i + 1),
                                                down_source(wd, 0, i), down_source(wd, 1, i))):
                        load_piece(base + 4 + j, i, source)
                load_piece(base + P_FFN - 2, 0, down_source(wd, 0, STEPS - 1))
                load_piece(base + P_FFN - 1, 0, down_source(wd, 1, STEPS - 1))

            def load_middle(layer):
                w_in = t["w_in"][layer].rearrange("(j k p) n -> p j k n", k=2, p=P)
                kv = t["mem_w_kv"][layer].rearrange("(h k p) n -> p h k n", h=2, p=P)
                w_out = t["w_out"][layer].rearrange("(k p) n -> p k n", p=P)
                wq = t["mem_w_q"][layer].rearrange("(h k p) n -> p h k n", h=2, p=P)
                wo = t["mem_w_o"][layer].rearrange("(k p) n -> p k n", p=P)
                for what, arg, n in layers[layer]:
                    if what == "in":
                        b, j = arg
                        load_piece(n["piece"], 0, w_in[:, j, :, b * HALF:(b + 1) * HALF])
                    elif what == "mem_k":
                        load_piece(n["piece"], 0, kv[:, arg, :, 0:256])
                    elif what == "mem_v":
                        load_piece(n["piece"], 0, kv[:, arg, :, 256:512])
                    elif what == "out":
                        load_piece(n["piece"], 0, w_out[:, arg:arg + 1, :])
                    elif what == "mem_q":
                        load_piece(n["piece"], 0, wq[:, arg, :, :])
                    elif what == "mem_o":
                        load_piece(n["piece"], 0, wo[:, arg:arg + 1, :])

            x = t["x"][0].rearrange("(t p) d -> p t d", p=P)
            for half in range(2):
                sp.dma_start(x_in[:, :, half * HALF:(half + 1) * HALF],
                             x[:, :, half * HALF:(half + 1) * HALF]).then_inc(x_loaded[half], 16)
            for layer in range(DEPTH):
                load_ffn(2 * layer)
                load_middle(layer)
                load_ffn(2 * layer + 1)
            sp.wait_ge(applied, n_heads)
            sp.dma_start(final_gain, t["final_norm"].partition_broadcast(P)).then_inc(final_loaded, 16)
            for j in range(2 * TT):
                tt, half = j // 2, j % 2
                sp.wait_ge(out_ready, j + 1)
                sp.dma_start(out[0, tt * P:(tt + 1) * P, half * HALF:(half + 1) * HALF],
                             out_rows[:, tt, half * HALF:(half + 1) * HALF]).then_inc(out_stored, 16)
            sp.wait_ge(out_stored, 16 * 2 * TT)

        @block.gpsimd
        def _(pool):
            count = [0]

            def link(ins):
                count[0] += 1
                ins.then_inc(pool_done, 1)
                pool.wait_ge(pool_done, count[0])

            def load(to, source, signal=params_loaded):
                pool.dma_start(to, source).then_inc(signal, 16)

            load(const[:, 0:K_ID], constants[:, 0:K_ID])
            for tt in range(TT):
                load(pos[:, tt:tt + 1], t["positions"][0, tt * P:(tt + 1) * P].unsqueeze(1))
            for j, name in enumerate(("q1", "k1", "q2", "k2")):
                load(lambdas[:, j, :, :].rearrange("p l d -> p (l d)"),
                     t[f"diff_lambda_{name}"].rearrange("l d -> (l d)").partition_broadcast(P))
            load(subln[:, :, :].rearrange("p l d -> p (l d)"),
                 t["diff_subln"].rearrange("l d -> (l d)").partition_broadcast(P))
            load(mem_rows, t["mem"][0].rearrange("(t p) d -> p t d", p=P), mem_loaded)

            def add_squares(stage):
                for p in range(4):
                    pool.wait_ge(x_squared, 4 * stage + p + 1)
                    pool.tensor_tensor(squares[:, 2 * p, :], squares[:, 2 * p, :], squares[:, 2 * p + 1, :],
                                       ALU.add).then_inc(squares_added, 1)

            for layer in range(DEPTH):
                add_squares(STAGES * layer)
                add_squares(STAGES * layer + 1)
                for what, arg, n in layers[layer]:
                    if what == "residual":
                        add_squares(STAGES * layer + 2)
                    if what != "rotate":
                        continue
                    first, heads, wide, rot, cos, sin, blocks = {
                        "a": (AQ, 4 * A_HEADS, A_MAP, ROT_A, cos_a, sin_a, 1),
                        "b": (BQ, 2 * B_HEADS, HD, ROT, cos_h, sin_h, 3),
                        "c": (CQ, 2 * C_HEADS, HD, ROT, cos_h, sin_h, 6)}[arg]
                    if layer == 0 and arg == "a":
                        pool.wait_ge(tables_ready, 1)
                    pool.wait_ge(rows0_stored, layer * BLOCKS + blocks)
                    pool.wait_ge(rows1_stored, layer * BLOCKS + blocks)
                    h = rot // 2
                    for tt in range(TT):
                        rows = qkv[:, tt, first:first + heads * wide].rearrange("p (h d) -> p h d", d=wide)
                        t1, t2 = (r[:, tt, 0:heads * rot].rearrange("p (h d) -> p h d", d=rot) for r in (rot_1, rot_2))
                        c = cos[:, tt, :].unsqueeze(1).broadcast_to([P, heads, rot])
                        s = sin[:, tt, :].unsqueeze(1).broadcast_to([P, heads, rot])
                        pool.tensor_tensor(t1, rows[:, :, 0:rot], c, ALU.mult)
                        pool.tensor_tensor(t2[:, :, 0:h], rows[:, :, h:rot], s[:, :, 0:h], ALU.mult)
                        link(pool.tensor_tensor(t2[:, :, h:rot], rows[:, :, 0:h], s[:, :, h:rot], ALU.mult))
                        last = pool.tensor_tensor(rows[:, :, 0:rot], t1, t2, ALU.add)
                        if tt < TT - 1:
                            link(last)
                    last.then_inc(rotated, 1)
                add_squares(STAGES * layer + 3)
            add_squares(LAST_STAGE)

        @block.scalar
        def _(act):
            def prepare(n, i=0, start=False):
                if isinstance(n, int) and not RING <= n < PIECES and not (n < RING and start):
                    return
                slot = n % RING
                act.wait_ge(weights_loaded[n % RAW], 16 * (n // RAW + 1) + 16 * (RING // RAW) * i)
                if n >= RING:
                    act.wait_ge(pieces_used, n - RING + 1 + RING * i)
                act.activation(w_hi[:, slot, :], w_raw[:, n % RAW, :], ACT.Copy).then_inc(pieces_rounded, 1)

            def ahead(n, count=1, i=0):
                for k in range(count):
                    prepare(n + k + RING, i)

            def columns(stage):
                for p in range(4):
                    act.wait_ge(x_updated, 4 * stage + p + 1)
                    if stage < LAST_STAGE:
                        act.activation(c_hi[:, 2 * p, :], x_cols[:, 2 * p, :], ACT.Copy,
                                       scale=stage_gain(stage, 2 * p))
                        act.activation(c_hi[:, 2 * p + 1, :], x_cols[:, 2 * p + 1, :], ACT.Copy,
                                       scale=stage_gain(stage, 2 * p + 1)).then_inc(cols_rounded, 1)
                    act.activation(squares[:, 2 * p:2 * p + 2, :], x_cols[:, 2 * p:2 * p + 2, :],
                                   ACT.Square).then_inc(x_squared, 1)

            def ffn(f):
                base = ffn_piece(f)
                s0 = f * STEPS

                def silu(s, i=0):
                    act.wait_ge(gates_scaled, s + 1 + i)
                    act.activation(gate[:, :], gate[:, :], ACT.Silu).then_inc(gates_active, 1)

                def round_hidden(s, i=0, used=None, to=h_hi):
                    act.wait_ge(hidden_ready, s + 1 + i)
                    if used is not None:
                        act.wait_ge(pieces_used, used + RING * i)
                    act.activation(to[:, :], hidden[:, :], ACT.Copy).then_inc(hidden_rounded, 1)

                ahead(base - 1, 3)
                act.wait_ge(rms_spread, f + 1)
                act.activation(rms_cols[:, :], bank[6][:, 0:SEQ], ACT.Copy).then_inc(rms_cols_ready, 1)
                silu(s0)
                ahead(base + 2, 2)
                round_hidden(s0)
                with act.Fori(0, STEPS - 2) as i:
                    n = base + 4
                    ahead(n, 2, i)
                    silu(s0 + 1, i)
                    ahead(n + 2, 4, i)
                    round_hidden(s0 + 1, i, n + 6)
                n = base + 4 + 6 * (STEPS - 2)
                ahead(n, 2)
                silu(s0 + STEPS - 1)
                ahead(n + 2, 2)
                round_hidden(s0 + STEPS - 1, to=last_hi)
                ahead(n + 4, 3)

            def middle(layer):
                for what, arg, n in layers[layer]:
                    if what in PIECE_EVENTS:
                        ahead(n["piece"] - 1)
                    if what == "store_in":
                        b = arg
                        act.wait_ge(rms_ready, STAGES * layer + 2)
                        act.wait_ge(pieces_used, last_piece(layer, "in", (b, 3)))
                        act.activation(qkv[:, 0, b * HALF:(b + 1) * HALF], bank[(2 * b) % 4][:, :], ACT.Copy,
                                       scale=rms[:, 3, 0:1]).then_inc(rows0_stored, 1)
                    elif what == "store_k":
                        act.wait_ge(pieces_used, last_piece(layer, "mem_k", 1))
                        act.activation(mem_k[:, :, :], bank[MEM_K][:, :].rearrange("p (k n) -> p k n", k=2),
                                       ACT.Copy).then_inc(mem_k_stored, 1)
                    elif what == "store_q":
                        act.wait_ge(pieces_used, last_piece(layer, "mem_q", 1))
                        act.activation(mem_q[:, :, :], bank[MEM_Q][:, :].rearrange("p (k n) -> p k n", k=2),
                                       ACT.Copy).then_inc(mem_q_stored, 1)
                    elif what == "tables":
                        act.wait_ge(angles_ready, 1)
                        act.activation(angle[:, 3, :, :, :], angle[:, 3, :, :, :], ACT.Sin).then_inc(sines_ready, 1)
                        act.wait_ge(lambdas_summed, 1)
                        act.activation(lam[:, 1, :, :], lam[:, 0, :, :], ACT.Exp).then_inc(lambdas_exp, 1)
                    elif what == "mem_norm":
                        act.wait_ge(mem_loaded, 16)
                        for tt in range(TT):
                            act.activation(probs[:, 2 * tt:2 * tt + 2, :].rearrange("p a b -> p (a b)"),
                                           mem_rows[:, tt, :], ACT.Square,
                                           accum_out=rms_a[:, 0, tt:tt + 1]).then_inc(mem_squared, 1)
                    elif what == "turn_mem":
                        act.wait_ge(mem_turned, arg + 1)
                        act.activation(mem_cols[:, 2 * arg:2 * arg + 2, :],
                                       bank[4 + arg % 2][:, :].rearrange("p (k n) -> p k n", k=2),
                                       ACT.Copy).then_inc(mem_cols_ready, 1)
                    elif what == "mem_gain":
                        if arg == 0:
                            act.wait_ge(mem_cols_ready, 4)
                        act.activation(m_hi[:, arg, :], mem_cols[:, arg, :], ACT.Copy,
                                       scale=gain_col(layer, 3, arg)).then_inc(mem_rounded, 1)
                    elif what == "turn_qk":
                        act.wait_ge(qk_turned, n["turn_qk"] + 1)
                        act.activation(qk_cols[:, 2 * arg:2 * arg + 2, :],
                                       bank[4 + n["turn_qk"] % 2][:, :].rearrange("p (k n) -> p k n", k=2),
                                       ACT.Copy).then_inc(qk_stored, 1)
                    elif what == "turn_mixed":
                        act.wait_ge(mixed_turned, n["turn_mixed"] + 1)
                        p = min(arg, 3)
                        act.activation(c_hi[:, 2 * p:2 * p + 2, :],
                                       bank[4 + n["turn_mixed"] % 2][:, :].rearrange("p (k n) -> p k n", k=2),
                                       ACT.Copy).then_inc(cols_rounded, 1)
                    elif what == "residual":
                        columns(STAGES * layer + arg)
                    elif what == "scores":
                        for j in range(len(arg.maps)):
                            m = n["map"] + j
                            wide = (128, 256) if arg.group != "m" else (256, 256)
                            act.wait_ge(masked, m + 1)
                            at = 0
                            for tt in range(TT):
                                view = probs[:, m % PLACES, at:at + wide[tt]]
                                total = sums[:, n["batch"] % 2, tt, arg.slot, j:j + 1]
                                if tt == 0 and j == 0 and arg.slot == 0 and n["batch"] >= 2:
                                    act.wait_ge(mixed_stored, n["batch"] - 1)
                                last = act.activation(view, view, ACT.Exp, scale=-1.0,
                                                      bias=bias[:, m % PLACES, tt:tt + 1], accum_out=total)
                                at += wide[tt]
                            last.then_inc(exped, 1)

            act.dma_start(const[:, K_ID:K_COLS], constants[:, K_ID:K_COLS]).then_inc(gains_loaded, 16)
            for which, name in enumerate(("ffn1_norm", "mix_norm", "memq_norm", "memkv_norm", "ffn2_norm")):
                at = which * DEPTH * KC
                act.dma_start(gain_rows[at:at + DEPTH * KC, :],
                              t[name].rearrange("l (k p) -> (l k) p", p=P)).then_inc(gains_loaded, 16)
            act.wait_ge(gains_turned, 1)
            act.activation(gains[:, :], bank[7][:, 0:10 * KC], ACT.Copy).then_inc(gains_ready, 1)
            act.wait_ge(gains_ready, 1)
            prepare(0, start=True)
            columns(0)
            for n in range(1, RING):
                prepare(n, start=True)

            for layer in range(DEPTH):
                if layer:
                    columns(STAGES * layer)
                ffn(2 * layer)
                columns(STAGES * layer + 1)
                middle(layer)
                columns(STAGES * layer + 3)
                ffn(2 * layer + 1)
            columns(LAST_STAGE)

        @block.vector
        def _(dve):
            count = [0]

            def link(ins):
                count[0] += 1
                ins.then_inc(vector_done, 1)
                dve.wait_ge(vector_done, count[0])

            def prepare(n, i=0, start=False):
                if isinstance(n, int) and not RING <= n < PIECES and not (n < RING and start):
                    return
                slot = n % RING
                dve.wait_ge(pieces_rounded, n + 1 + RING * i)
                dve.tensor_tensor(w_lo[:, slot, :], w_raw[:, n % RAW, :], raw(w_hi[:, slot, :]),
                                  ALU.subtract).then_inc(pieces_split, 1)

            def ahead(n, count=1, i=0):
                for k in range(count):
                    prepare(n + k + RING, i)

            def rsqrt(y, source, total, tmp, width, final):
                link(dve.tensor_scalar(total, source, 1.0 / width, EPS, ALU.mult, ALU.add))
                link(dve.tensor_scalar(y.bitcast(I32), total.bitcast(I32), -0.5, float(0x5F3759DF),
                                       ALU.mult, ALU.add))
                for k in range(3):
                    link(dve.scalar_tensor_tensor(tmp, y, -0.5, y, ALU.mult, ALU.mult))
                    link(dve.tensor_tensor(tmp, tmp, total, ALU.mult))
                    last = dve.scalar_tensor_tensor(y, tmp, 1.5, y, ALU.add, ALU.mult)
                    if k < 2 or final is None:
                        link(last)
                    else:
                        last.then_inc(final, 1)

            def norm(stage):
                dve.wait_ge(squares_summed, stage + 1)
                rsqrt(rms[:, 3, :], bank[6][:, 0:TT], rms[:, 0, :], rms[:, 2, :], D, rms_ready)
                dve.wait_ge(rms_ready, stage + 1)

            def spread(f):
                dve.tensor_scalar(diag[:, 0, :], ident, rms[:, 3, 0:1], None, ALU.mult)
                dve.tensor_scalar(diag[:, 1, :], ident, rms[:, 3, 1:2], None, ALU.mult).then_inc(diag_ready, 1)

            def residual(stage, first=None):
                for p in range(5):
                    if p < 4:
                        dve.wait_ge(*ready_quarter(stage, p))
                        x = x_cols[:, 2 * p:2 * p + 2, :]
                        b = bank[p][:, :].rearrange("p (k n) -> p k n", k=2)
                        if stage:
                            dve.tensor_tensor(x, b, x, ALU.add).then_inc(x_updated, 1)
                        else:
                            dve.tensor_copy(x, b).then_inc(x_updated, 1)
                    if p and first is not None:
                        q = p - 1
                        dve.wait_ge(x_updated, 4 * stage + q + 1)
                        dve.wait_ge(cols_rounded, first + q + 1)
                        for k in (2 * q, 2 * q + 1):
                            last = dve.scalar_tensor_tensor(c_lo[:, k, :], x_cols[:, k, :], stage_gain(stage, k),
                                                            raw(c_hi[:, k, :]), ALU.mult, ALU.subtract)
                        last.then_inc(cols_split, 1)

            def ffn(f):
                base = ffn_piece(f)
                s0 = f * STEPS

                def scale_gate(s, used, i=0):
                    dve.wait_ge(pieces_used, used + RING * i)
                    dve.tensor_tensor(gate[:, :].rearrange("p (c n) -> p c n", c=2),
                                      bank[GATE][:, :].rearrange("p (c n) -> p c n", c=2),
                                      rms_cols[:, :].unsqueeze(1).broadcast_to([P, 2, SEQ]),
                                      ALU.mult).then_inc(gates_scaled, 1)

                def multiply(s, used, i=0):
                    dve.wait_ge(gates_active, s + 1 + i)
                    dve.scalar_tensor_tensor(gate[:, :].rearrange("p (c n) -> p c n", c=2),
                                             gate[:, :].rearrange("p (c n) -> p c n", c=2), 0.5,
                                             rms_cols[:, :].unsqueeze(1).broadcast_to([P, 2, SEQ]),
                                             ALU.mult, ALU.mult).then_inc(gates_weighted, 1)
                    dve.wait_ge(pieces_used, used + RING * i)
                    dve.wait_ge(gates_weighted, s + 1 + i)
                    dve.tensor_tensor(hidden[:, :], bank[UP][:, :], gate[:, :], ALU.mult).then_inc(hidden_ready, 1)

                def split_hidden(s, i=0, hi=h_hi, lo=h_lo):
                    dve.wait_ge(hidden_rounded, s + 1 + i)
                    dve.tensor_tensor(lo[:, :], hidden[:, :], raw(hi[:, :]),
                                      ALU.subtract).then_inc(hidden_split, 1)

                ahead(base - 1, 2)
                norm(f // 2 * STAGES + f % 2 * 3)
                spread(f)
                ahead(base + 1, 1)
                dve.wait_ge(rms_cols_ready, f + 1)
                scale_gate(s0, base + 2)
                ahead(base + 2, 1)
                multiply(s0, base + 4)
                ahead(base + 3, 1)
                split_hidden(s0)
                with dve.Fori(0, STEPS - 2) as i:
                    n = base + 4
                    scale_gate(s0 + 1, n + 2, i)
                    ahead(n, 3, i)
                    multiply(s0 + 1, n + 4, i)
                    ahead(n + 3, 3, i)
                    split_hidden(s0 + 1, i)
                n = base + 4 + 6 * (STEPS - 2)
                scale_gate(s0 + STEPS - 1, n + 2)
                ahead(n, 3)
                multiply(s0 + STEPS - 1, n + 4)
                ahead(n + 3, 1)
                split_hidden(s0 + STEPS - 1, hi=last_hi, lo=last_lo)
                ahead(n + 4, 3)

            def finish_a(layer, n):
                b = bank[7][:, :].rearrange("p (t h d) -> p t h d", t=TT, h=A_HEADS)
                link(dve.tensor_copy(out_a[:, :, :, :], b))
                link(dve.tensor_tensor(sq_a[:, :, :, :], out_a[:, :, :, :], out_a[:, :, :, :], ALU.mult))
                link(dve.tensor_reduce(rms_a[:, 0, :], sq_a[:, :, :, :].rearrange("p t h d -> p (t h) d"),
                                       AX.X, ALU.add))
                rsqrt(rms_a[:, 3, :], rms_a[:, 0, :], rms_a[:, 0, :], rms_a[:, 2, :], HD, None)
                flat = out_a[:, :, :, :].rearrange("p t h d -> p (t h) d")
                factor = rms_a[:, 3, :].unsqueeze(2).broadcast_to([P, TT * A_HEADS, HD])
                link(dve.tensor_tensor(flat, flat, factor, ALU.mult))
                g = subln[:, layer, :].unsqueeze(1).broadcast_to([P, A_HEADS, HD])
                for tt in range(TT):
                    last = dve.tensor_tensor(mixed[:, tt, 0:A_HEADS * HD].rearrange("p (h d) -> p h d", d=HD),
                                             out_a[:, tt, :, :], g, ALU.mult)
                last.then_inc(mixed_stored, 1)

            def middle(layer):
                for what, arg, n in layers[layer]:
                    if what in PIECE_EVENTS:
                        ahead(n["piece"] - 1)
                    if what == "store_in":
                        b = arg
                        dve.wait_ge(pieces_used, last_piece(layer, "in", (b, 3)))
                        dve.tensor_scalar(qkv[:, 1, b * HALF:(b + 1) * HALF], bank[(2 * b + 1) % 4][:, :],
                                          rms[:, 3, 1:2], None, ALU.mult).then_inc(rows1_stored, 1)
                    elif what == "store_v":
                        dve.wait_ge(pieces_used, last_piece(layer, "mem_v", 1))
                        dve.tensor_copy(mem_v[:, :, :], bank[MEM_V][:, :].rearrange("p (k n) -> p k n", k=2))\
                           .then_inc(mem_v_stored, 1)
                    elif what == "tables":
                        tables()
                    elif what == "mem_norm":
                        dve.wait_ge(mem_squared, TT)
                        rsqrt(rms_a[:, 3, 0:TT], rms_a[:, 0, 0:TT], rms_a[:, 0, 0:TT], rms_a[:, 2, 0:TT], D, None)
                        for tt in range(TT):
                            last = dve.tensor_scalar(mem_rows[:, tt, :], mem_rows[:, tt, :], rms_a[:, 3, tt:tt + 1],
                                                     None, ALU.mult)
                        last.then_inc(mem_scaled, 1)
                    elif what == "mem_gain":
                        dve.wait_ge(mem_rounded, layer * KC + arg + 1)
                        dve.scalar_tensor_tensor(m_lo[:, arg, :], mem_cols[:, arg, :], gain_col(layer, 3, arg),
                                                 raw(m_hi[:, arg, :]), ALU.mult, ALU.subtract).then_inc(mem_split, 1)
                    elif what == "norm":
                        norm(STAGES * layer + arg)
                        if arg == 2:
                            link(dve.tensor_scalar(rms_scaled[:, :], rms[:, 3, :], -HD ** -0.5, None, ALU.mult))
                    elif what == "residual":
                        residual(STAGES * layer + arg, layer * T_LAYER + T_MQ)
                    elif what == "turn_mixed":
                        first = layer * T_LAYER + (T_MO if arg == 4 else T_OUT + arg)
                        dve.wait_ge(cols_rounded, first + 1)
                        p = min(arg, 3)
                        b = bank[4 + n["turn_mixed"] % 2][:, :].rearrange("p (k n) -> p k n", k=2)
                        dve.tensor_tensor(c_lo[:, 2 * p:2 * p + 2, :], b, raw(c_hi[:, 2 * p:2 * p + 2, :]),
                                          ALU.subtract).then_inc(cols_split, 1)
                    elif what == "scores":
                        for j in range(len(arg.maps)):
                            m = n["map"] + j
                            dve.wait_ge(scored, m + 1)
                            if m >= PLACES:
                                dve.wait_ge(probs_turned, place_free[m])
                            wide = (128, 256) if arg.group != "m" else (256, 256)
                            at = 0
                            for tt in range(TT):
                                if arg.group == "m":
                                    mask, scale = const[:, K_ZERO:K_ZERO + 256], rms_scaled[:, tt:tt + 1]
                                else:
                                    mask = const[:, arg.mask + at:arg.mask + at + wide[tt]]
                                    scale = -(len(arg.maps) / HD) ** 0.5
                                last = dve.tensor_tensor_reduce(
                                    probs[:, m % PLACES, at:at + wide[tt]], bank[4 + m % 2][:, at:at + wide[tt]], mask,
                                    scale, BIG, ALU.add, ALU.min, bias[:, m % PLACES, tt:tt + 1])
                                at += wide[tt]
                            last.then_inc(masked, 1)
                    elif what == "turn":
                        h = n["head"]
                        dve.wait_ge(probs_turned, h + 1)
                        if h >= 2:
                            dve.wait_ge(applied, h - 1)
                        wide = 384 if arg.group != "m" else 512
                        dve.tensor_copy(probs_t[:, h % 2, 0:wide], bank[6][:, 0:wide]).then_inc(probs_stored, 1)
                    elif what == "combine":
                        combine(arg, n, layer)
                    elif what == "apply" and arg.last:
                        dve.wait_ge(applied, n["head"] + 1)
                        if arg.group == "a":
                            finish_a(layer, n)
                            continue
                        nh, half = arg.batch, n["batch"] % 2
                        dve.wait_ge(exped, n["map"] + 1)
                        link(dve.reciprocal(recips[:, half, :, 0:nh, 0], sums[:, half, :, 0:nh, 0]))
                        first = {"b": 256, "c": 640, "m": 0}[arg.group] + (arg.h - nh + 1) * HD
                        for tt in range(TT):
                            last = dve.tensor_tensor(
                                mixed[:, tt, first:first + nh * HD].rearrange("p (h d) -> p h d", d=HD),
                                bank[7][:, tt * nh * HD:(tt + 1) * nh * HD].rearrange("p (h d) -> p h d", d=HD),
                                recips[:, half, tt, 0:nh, 0].unsqueeze(2).broadcast_to([P, nh, HD]), ALU.mult)
                        last.then_inc(mixed_stored, 1)

            def combine(arg, n, layer):
                m, half, s = n["map"], n["batch"] % 2, arg.slot
                dve.wait_ge(exped, m + 2)
                link(dve.reciprocal(recips[:, half, :, s, :], sums[:, half, :, s, :]))
                link(dve.tensor_scalar(recips[:, half, :, s, 1], recips[:, half, :, s, 1], lam[:, 3, layer, 0:1],
                                       None, ALU.mult))
                for tt, (a, b) in enumerate(((0, 128), (128, 384))):
                    p1, p2 = probs[:, m % PLACES, a:b], probs[:, (m + 1) % PLACES, a:b]
                    link(dve.tensor_scalar(p2, p2, recips[:, half, tt, s, 1:2], None, ALU.mult))
                    last = dve.scalar_tensor_tensor(p1, p1, recips[:, half, tt, s, 0:1], p2, ALU.mult, ALU.add)
                last.then_inc(combined, 1)

            def tables():
                dve.wait_ge(params_loaded, 16 * N_PARAMS)
                link(dve.tensor_copy(pos_f[:, :], pos[:, :]))
                freq = const[:, K_FREQ:K_FREQ + NF]
                for tt in range(TT):
                    for part in range(2):
                        last = dve.tensor_scalar(angle[:, 0, part, tt, :], freq, pos_f[:, tt:tt + 1], None, ALU.mult)
                link(last)
                magic = 1.5 * 2.0 ** 23
                for part in range(2):
                    link(dve.tensor_scalar(angle[:, 1, part, :, :], angle[:, 0, part, :, :], 1 / (2 * math.pi),
                                           0.25 * part, ALU.mult, ALU.add))
                link(dve.tensor_scalar(angle[:, 1, :, :, :], angle[:, 1, :, :, :], magic, None, ALU.add))
                link(dve.tensor_scalar(angle[:, 1, :, :, :], angle[:, 1, :, :, :], -magic, None, ALU.add))
                c1 = 6.28125
                c2 = float(np.float32(round((2 * math.pi - c1) * 2 ** 20) / 2 ** 20))
                c3 = 2 * math.pi - c1 - c2
                source = angle[:, 0, :, :, :]
                for c in (c1, c2, c3):
                    link(dve.scalar_tensor_tensor(angle[:, 3, :, :, :].rearrange("p a t f -> p (a t f)"),
                                                  angle[:, 1, :, :, :].rearrange("p a t f -> p (a t f)"), -c,
                                                  source.rearrange("p a t f -> p (a t f)"), ALU.mult, ALU.add))
                    source = angle[:, 3, :, :, :]
                link(dve.tensor_scalar(angle[:, 3, 1, :, :], angle[:, 3, 1, :, :], math.pi / 2, None, ALU.add))
                dve.tensor_scalar(angle[:, 3, :, :, :], angle[:, 3, :, :, :], 3.1415925, -3.1415925,
                                  ALU.min, ALU.max).then_inc(angles_ready, 1)
                for j in range(2):
                    link(dve.tensor_tensor(lambdas[:, 2 * j, :, :], lambdas[:, 2 * j, :, :], lambdas[:, 2 * j + 1, :, :],
                                           ALU.mult))
                    last = dve.tensor_reduce(lam[:, 0, j, :], lambdas[:, 2 * j, :, :], AX.X, ALU.add)
                    if j == 0:
                        link(last)
                last.then_inc(lambdas_summed, 1)
                for layer in range(DEPTH):
                    init = 0.8 - 0.6 * math.exp(-0.3 * layer)
                    link(dve.tensor_scalar(subln[:, layer, :], subln[:, layer, :], 1.0 - init, None, ALU.mult))
                dve.wait_ge(lambdas_exp, 1)
                for layer in range(DEPTH):
                    init = 0.8 - 0.6 * math.exp(-0.3 * layer)
                    link(dve.tensor_tensor(lam[:, 2, layer, 0:1], lam[:, 1, 1, layer:layer + 1],
                                           lam[:, 1, 0, layer:layer + 1], ALU.subtract))
                    link(dve.tensor_scalar(lam[:, 3, layer, 0:1], lam[:, 2, layer, 0:1], -init, None, ALU.add))
                dve.wait_ge(sines_ready, 1)
                for part, (head, small) in enumerate(((sin_h, sin_a), (cos_h, cos_a))):
                    for table, at, n in ((head, 0, ROT // 2), (small, ROT // 2, ROT_A // 2)):
                        value = angle[:, 3, part, :, at:at + n]
                        dve.tensor_scalar(table[:, :, 0:n], value, 1.0 if part else -1.0, None, ALU.mult)
                        last = dve.tensor_copy(table[:, :, n:2 * n], value)
                last.then_inc(tables_ready, 1)

            dve.wait_ge(gains_ready, 1)
            residual(0, 0)
            for n in range(RING):
                prepare(n, start=True)

            for layer in range(DEPTH):
                if layer:
                    residual(STAGES * layer, layer * T_LAYER + T_FFN1)
                ffn(2 * layer)
                residual(STAGES * layer + 1, layer * T_LAYER + T_MIX)
                middle(layer)
                residual(STAGES * layer + 3, layer * T_LAYER + T_FFN2)
                ffn(2 * layer + 1)
            residual(LAST_STAGE)
            norm(LAST_STAGE)
            dve.wait_ge(final_loaded, 16)
            for j in range(2 * TT):
                tt, half = j // 2, j % 2
                dve.wait_ge(out_turned, 1)
                at = slice(half * HALF, (half + 1) * HALF)
                dve.scalar_tensor_tensor(out_rows[:, tt, at], bank[OUT_BANKS[tt][half]][:, :], rms[:, 3, tt:tt + 1],
                                         final_gain[:, at], ALU.mult, ALU.mult).then_inc(out_ready, 1)

        @block.tensor
        def _(pe):
            reader = {}

            def claim(b):
                if b in reader:
                    pe.wait_ge(*reader[b])

            def three(out_, lhs, rhs, start, stop):
                (lh, ll), (rh, rl) = lhs, rhs
                pe.matmul(out_, lh, rh, start=start, stop=False, skip_group_check=True)
                pe.matmul(out_, ll, rh, start=False, stop=False, skip_group_check=True)
                return pe.matmul(out_, lh, rl, start=False, stop=stop, skip_group_check=True)

            def w(slot, a, b):
                return w_hi[:, slot, a:b], w_lo[:, slot, a:b]

            def col(kc, a, b):
                return c_hi[:, kc, a:b], c_lo[:, kc, a:b]

            def signal(ins, c, closing):
                if c == KC - 1:
                    ins.then_inc(pieces_used, 1)
                elif closing and c % 2:
                    ins.then_inc(quarter_done, 1)

            def sum_squares(stage):
                pe.wait_ge(squares_added, 4 * stage + 4)
                claim(6)
                for tt in range(TT):
                    for p in range(4):
                        last = pe.matmul(bank[6][:, tt:tt + 1], squares[:, 2 * p, tt * P:(tt + 1) * P],
                                         const[:, K_ONE:K_ONE + 1], start=p == 0, stop=p == 3)
                last.then_inc(squares_summed, 1)
                reader[6] = (rms_ready, stage + 1)

            def updates(stage):
                for b in range(4):
                    reader[b] = (x_updated, 4 * stage + b + 1)

            def ffn(f, cols_at):
                base = ffn_piece(f)
                s0 = f * STEPS

                def columns(n, b, i=0, wait_cols=False, halves=(0, 1)):
                    for half in halves:
                        slot = (n + half) % RING
                        pe.wait_ge(pieces_split, n + half + 1 + RING * i)
                        for k in range(4):
                            kc = 4 * half + k
                            if wait_cols and k % 2 == 0:
                                pe.wait_ge(cols_split, cols_at + kc // 2 + 1)
                            for fc in range(2):
                                at = k * 256 + fc * P
                                last = three(bank[b][:, fc * 256:(fc + 1) * 256], w(slot, at, at + P),
                                             col(kc, 0, SEQ), start=(kc == 0 and fc == 0),
                                             stop=(kc == KC - 1))
                        last.then_inc(pieces_used, 1)

                def down(n, s, first, final, i=0, hi=h_hi, lo=h_lo):
                    pe.wait_ge(hidden_split, s + 1 + i)
                    if first:
                        for b in range(4):
                            claim(b)
                    for half in range(2):
                        slot = (n + half) % RING
                        pe.wait_ge(pieces_split, n + half + 1 + RING * i)
                        for c in range(KC):
                            at = c % 2 * SEQ
                            last = three(bank[c // 2][:, at:at + SEQ], w(slot, c * P, (c + 1) * P),
                                         (hi[:, half * SEQ:(half + 1) * SEQ], lo[:, half * SEQ:(half + 1) * SEQ]),
                                         start=first and half == 0 and c % 2 == 0, stop=final and half == 1)
                            signal(last, c, final and half == 1)

                claim(GATE)
                columns(base, GATE, wait_cols=True)
                sum_squares(f // 2 * STAGES + f % 2 * 3)
                claim(UP)
                columns(base + 2, UP, halves=(0,))
                pe.wait_ge(diag_ready, f + 1)
                claim(6)
                for tt in range(TT):
                    last = pe.matmul(bank[6][:, tt * P:(tt + 1) * P], const[:, K_ONE:K_ONE + P], diag[:, tt, :],
                                     start=True, stop=True)
                last.then_inc(rms_spread, 1)
                reader[6] = (rms_cols_ready, f + 1)
                columns(base + 2, UP, halves=(1,))
                pe.wait_ge(gates_scaled, s0 + 1)
                columns(base + 4, GATE)
                pe.wait_ge(hidden_ready, s0 + 1)
                columns(base + 6, UP)
                down(base + 8, s0, True, False)
                with pe.Fori(0, STEPS - 2) as i:
                    n = base + 10
                    pe.wait_ge(gates_scaled, s0 + 2 + i)
                    columns(n, GATE, i)
                    pe.wait_ge(hidden_ready, s0 + 2 + i)
                    columns(n + 2, UP, i)
                    down(n + 4, s0 + 1, False, False, i)
                down(base + P_FFN - 2, s0 + STEPS - 1, False, True, hi=last_hi, lo=last_lo)
                reader[GATE] = (gates_scaled, s0 + STEPS)
                reader[UP] = (hidden_ready, s0 + STEPS)

            def half_product(n, half, b, lhs, rhs, ready):
                pe.wait_ge(pieces_split, n + 1)
                for k in range(4):
                    kc = 4 * half + k
                    pe.wait_ge(*ready(kc))
                    for j in range(2):
                        last = three(bank[b][:, j * 256:(j + 1) * 256], lhs(k, kc, j), rhs(k, kc, j),
                                     start=(kc == 0 and j == 0), stop=(kc == KC - 1))
                last.then_inc(pieces_used, 1)

            def full_product(n, kc, first, final):
                pe.wait_ge(pieces_split, n + 1)
                for c in range(KC):
                    if first and c % 2 == 0:
                        claim(c // 2)
                    at = c % 2 * SEQ
                    last = three(bank[c // 2][:, at:at + SEQ], w(n % RING, c * P, (c + 1) * P), col(kc, 0, SEQ),
                                 start=first and c % 2 == 0, stop=final)
                    signal(last, c, final)

            def middle(layer):
                c0 = layer * T_LAYER
                for what, arg, n in layers[layer]:
                    if what == "in":
                        b, j = arg
                        piece = n["piece"]
                        pe.wait_ge(pieces_split, piece + 1)
                        if b == 0:
                            pe.wait_ge(cols_split, c0 + T_MIX + j + 1)
                        for k in range(2):
                            for tt in range(TT):
                                if j == 0 and k == 0:
                                    claim((2 * b + tt) % 4)
                                last = three(bank[(2 * b + tt) % 4][:, :], col(2 * j + k, tt * P, (tt + 1) * P),
                                             w(piece % RING, k * HALF, (k + 1) * HALF),
                                             start=(j == 0 and k == 0), stop=(j == 3 and k == 1))
                        last.then_inc(pieces_used, 1)
                        if j == 3:
                            reader[(2 * b) % 4] = (rows0_stored, layer * BLOCKS + b + 1)
                            reader[(2 * b + 1) % 4] = (rows1_stored, layer * BLOCKS + b + 1)
                    elif what == "norm":
                        sum_squares(STAGES * layer + arg)
                    elif what == "turn_mem":
                        b = 4 + arg % 2
                        pe.wait_ge(mem_scaled, 1)
                        claim(b)
                        for k in range(2):
                            for tt in range(TT):
                                at = k * 256 + tt * P
                                last = pe.transpose(bank[b][:, at:at + P],
                                                    mem_rows[:, tt, (2 * arg + k) * P:(2 * arg + k + 1) * P], ident)
                        last.then_inc(mem_turned, 1)
                        reader[b] = (mem_cols_ready, arg + 1)
                    elif what == "mem_k":
                        slot = n["piece"] % RING
                        if arg == 0:
                            claim(MEM_K)
                        half_product(n["piece"], arg, MEM_K, lambda k, kc, j: w(slot, k * 256 + j * P, k * 256 + (j + 1) * P),
                                     lambda k, kc, j: (m_hi[:, kc, :], m_lo[:, kc, :]),
                                     lambda kc: (mem_split, layer * KC + kc + 1))
                        reader[MEM_K] = (mem_k_stored, layer + 1)
                    elif what == "mem_v":
                        slot = n["piece"] % RING
                        if arg == 0:
                            claim(MEM_V)
                        half_product(n["piece"], arg, MEM_V,
                                     lambda k, kc, j: (m_hi[:, kc, j * P:(j + 1) * P], m_lo[:, kc, j * P:(j + 1) * P]),
                                     lambda k, kc, j: w(slot, k * 256, (k + 1) * 256),
                                     lambda kc: (mem_split, layer * KC + kc + 1))
                        reader[MEM_V] = (mem_v_stored, layer + 1)
                    elif what == "mem_q":
                        slot = n["piece"] % RING
                        if arg == 0:
                            claim(MEM_Q)
                        half_product(n["piece"], arg, MEM_Q, lambda k, kc, j: w(slot, k * 256 + j * P, k * 256 + (j + 1) * P),
                                     lambda k, kc, j: col(kc, 0, SEQ),
                                     lambda kc: (cols_split, c0 + T_MQ + kc // 2 + 1))
                        reader[MEM_Q] = (mem_q_stored, layer + 1)
                    elif what == "out":
                        pe.wait_ge(cols_split, c0 + T_OUT + arg // 2 + 1)
                        full_product(n["piece"], arg, arg == 0, arg == KC - 1)
                    elif what == "mem_o":
                        pe.wait_ge(cols_split, c0 + T_MO + 1)
                        full_product(n["piece"], KC - 2 + arg, arg == 0, arg == 1)
                    elif what == "residual":
                        updates(STAGES * layer + arg)
                    elif what == "turn_mixed":
                        b = 4 + n["turn_mixed"] % 2
                        pe.wait_ge(mixed_stored, layer * BATCHES + (1, 3, 4, 5, 6)[arg])
                        claim(b)
                        for k in range(2):
                            first = (2 * (arg % 4) + k) * P
                            for tt in range(TT):
                                at = k * 256 + tt * P
                                last = pe.transpose(bank[b][:, at:at + P], mixed[:, tt, first:first + P], ident)
                        last.then_inc(mixed_turned, 1)
                        reader[b] = (cols_split, c0 + (T_MO if arg == 4 else T_OUT + arg) + 1)
                    elif what == "turn_qk":
                        pe.wait_ge(rotated, layer * 3 + {0: 1, 1: 1, 2: 2, 3: 2, 4: 2}.get(arg, 3))
                        b = 4 + n["turn_qk"] % 2
                        claim(b)
                        for k in range(2):
                            blk = 2 * arg + k
                            first = blk * P if blk < 4 else (BQ + (blk - 4) * P if blk < 10 else CQ + (blk - 10) * P)
                            for tt in range(TT):
                                at = k * 256 + tt * P
                                last = pe.transpose(bank[b][:, at:at + P], qkv[:, tt, first:first + P], ident)
                        last.then_inc(qk_turned, 1)
                        reader[b] = (qk_stored, n["turn_qk"] + 1)
                    elif what == "scores":
                        mem = arg.group == "m"
                        if mem and arg.h == 0:
                            pe.wait_ge(mem_q_stored, layer + 1)
                            pe.wait_ge(mem_k_stored, layer + 1)
                        elif arg.h == 0:
                            pe.wait_ge(qk_stored, layer * 8 + {"a": 2, "b": 5, "c": 8}[arg.group])
                        for j, (qb, kb, p0, ps) in enumerate(arg.maps):
                            m = n["map"] + j
                            b = 4 + m % 2
                            claim(b)
                            at = 0
                            for tt in range(TT):
                                keys = 256 if mem else (tt + 1) * P
                                q, k = (mem_q, mem_k) if mem else (qk_cols, qk_cols)
                                last = pe.matmul(bank[b][:, at:at + keys], q[p0:p0 + ps, qb, tt * P:(tt + 1) * P],
                                                 k[p0:p0 + ps, kb, 0:keys], start=True, stop=True)
                                at += keys
                            last.then_inc(scored, 1)
                            reader[b] = (masked, m + 1)
                    elif what == "turn":
                        h, m = n["head"], n["map"]
                        if arg.group == "a":
                            pe.wait_ge(combined, layer * A_HEADS + arg.h + 1)
                        else:
                            pe.wait_ge(exped, m + 1)
                        claim(6)
                        for k in range(4 if arg.group == "m" else 3):
                            last = pe.transpose(bank[6][:, k * P:(k + 1) * P], probs[:, m % PLACES, k * P:(k + 1) * P], ident)
                        last.then_inc(probs_turned, 1)
                        reader[6] = (probs_stored, h + 1)
                    elif what == "apply":
                        h = n["head"]
                        pe.wait_ge(probs_stored, h + 1)
                        if arg.slot == 0:
                            claim(7)
                            if arg.group == "m":
                                pe.wait_ge(mem_v_stored, layer + 1)
                            else:
                                stored = layer * BLOCKS + {"a": 2, "b": 4, "c": 6}[arg.group]
                                pe.wait_ge(rows0_stored, stored)
                                pe.wait_ge(rows1_stored, stored)
                        for tt in range(TT):
                            at = (tt * arg.batch + arg.slot) * HD
                            if arg.group == "m":
                                terms = [(2 * tt, 0), (2 * tt + 1, 1)]
                            else:
                                terms = [(0, 0)] if tt == 0 else [(1, 0), (2, 1)]
                            for k, (blk, vt) in enumerate(terms):
                                v = mem_v if arg.group == "m" else qkv
                                last = pe.matmul(bank[7][:, at:at + HD], probs_t[:, h % 2, blk * P:(blk + 1) * P],
                                                 v[:, vt, arg.v_col:arg.v_col + HD],
                                                 start=k == 0, stop=k == len(terms) - 1)
                        last.then_inc(applied, 1)
                        if arg.last:
                            reader[7] = (mixed_stored, n["batch"] + 1)

            pe.wait_ge(gains_loaded, 16 * N_GAINS)
            pe.transpose(bank[7][:, 0:10 * KC], gain_rows[:, :], const[0:10 * KC, K_ID:K_ID + 10 * KC])\
              .then_inc(gains_turned, 1)
            reader[7] = (gains_ready, 1)
            for p in range(4):
                pe.wait_ge(x_loaded[p // 2], 16)
                for k in range(2):
                    for tt in range(TT):
                        at = k * 256 + tt * P
                        last = pe.transpose(bank[p][:, at:at + P], x_in[:, tt, (2 * p + k) * P:(2 * p + k + 1) * P],
                                            ident)
                last.then_inc(x_turned, 1)
            updates(0)
            for layer in range(DEPTH):
                ffn(2 * layer, layer * T_LAYER + T_FFN1)
                updates(STAGES * layer + 1)
                middle(layer)
                updates(STAGES * layer + 3)
                ffn(2 * layer + 1, layer * T_LAYER + T_FFN2)
                updates(STAGES * layer + 4)
            for half in range(2):
                for tt in range(TT):
                    claim(OUT_BANKS[tt][half])
                for k in range(4):
                    c = 4 * half + k
                    if k % 2 == 0:
                        pe.wait_ge(x_updated, 4 * LAST_STAGE + c // 2 + 1)
                    for tt in range(TT):
                        last = pe.transpose(bank[OUT_BANKS[tt][half]][:, k * P:(k + 1) * P],
                                            x_cols[:, c, tt * P:(tt + 1) * P], ident)
            last.then_inc(out_turned, 1)
            sum_squares(LAST_STAGE)


_INS = ["x", "mem", "positions", "ffn1_norm", "ffn1_w_gate", "ffn1_w_up", "ffn1_w_down", "mix_norm", "w_in", "w_out",
        "diff_lambda_q1", "diff_lambda_k1", "diff_lambda_q2", "diff_lambda_k2", "diff_subln", "memq_norm",
        "memkv_norm", "mem_w_q", "mem_w_kv", "mem_w_o", "ffn2_norm", "ffn2_w_gate", "ffn2_w_up", "ffn2_w_down",
        "final_norm"]


def kernel(**inputs):
    import concourse.bacc as bacc
    from concourse.bass_utils import run_bass_kernel_spmd

    nc = bacc.Bacc("TRN2", target_bir_lowering=False, num_devices=1)
    arrays, t = {}, {}

    def add(name, a):
        arrays[f"in_{name}_dram"] = a
        return nc.dram_tensor(f"in_{name}_dram", a.shape, mybir.dt.from_np(a.dtype), kind="ExternalInput").ap()

    for name in _INS:
        t[name] = add(name, np.ascontiguousarray(inputs[name]))
    constants = add("shape_constants", shape_constants())
    out = nc.dram_tensor("out_0_dram", (1, SEQ, D), F32, kind="ExternalOutput").ap()
    decoder_trunk(nc, t, constants, out)
    r = run_bass_kernel_spmd(nc, [arrays], core_ids=[0])
    return r.results[0]["out_0_dram"]
```

```python
import math
from contextlib import ExitStack

import numpy as np

import concourse.bass as bass
from concourse import mybir

F32 = mybir.dt.float32
F32R = mybir.dt.float32r
I32 = mybir.dt.int32
ALU = mybir.AluOpType
ACT = mybir.ActivationFunctionType
AX = mybir.AxisListType

P = 128
D = 1024
SEQ = 256
MEM = 256
DEPTH = 2
FF = 2816
HD = 64
A_HEADS, B_HEADS, C_HEADS = 4, 6, 6
A_MAP = HD // 2
MEM_HEADS = 4
EPS = 1e-6
NEG = -1e30
BIG = 3e38
ROPE_THETA = 500000.0
BRANCHES = ((128, 1), (512, 4), (2048, 16))

TT = SEQ // P
KC = D // P
PIECE = 1024
RING = 6
RAW = 3
STEPS = FF // 256
HALF = 512

AQ, AK, AV = 0, 256, 512
BQ, BK, BV = 768, 1152, 1536
CQ, CK, CV = 1920, 2304, 2688
BLOCKS = 3 * D // HALF
PLACES = 6
SCALAR_STORES = (2, 3)

P_FFN = 6 * STEPS
P_MID = 40
P_FFN2 = P_FFN + P_MID
P_LAYER = P_FFN2 + P_FFN
PIECES = DEPTH * P_LAYER

STAGES = 4
LAST_STAGE = STAGES * DEPTH
T_FFN1, T_MIX, T_OUT, T_MQ, T_MO, T_FFN2, T_LAYER = 0, 8, 16, 24, 32, 34, 42

ROT, ROT_A = HD // 4, A_MAP // 4
NF = ROT // 2 + ROT_A // 2

N_PARAMS = 1 + TT + 4 + 1
N_GAINS = 5

K_CAUSAL, K_DILATED, K_ZERO, K_ID, K_ONE, K_FREQ = 0, 384, 768, 1024, 1152, 1280
K_COLS = K_FREQ + NF


def shape_constants():
    out = np.zeros((P, K_COLS), np.float32)
    for tile, first, keys in ((0, 0, 128), (1, 128, 256)):
        delta = (tile * P + np.arange(P))[:, None] - np.arange(keys)[None, :]
        count = np.zeros(delta.shape)
        for window, dilation in BRANCHES:
            count += (delta >= 0) & (delta % dilation == 0) & (delta <= window)
        out[:, K_CAUSAL + first:K_CAUSAL + first + keys] = np.where(delta >= 0, 0.0, NEG)
        out[:, K_DILATED + first:K_DILATED + first + keys] = np.where(
            count > 0, math.sqrt(HD) * np.log(np.maximum(count, 1)), NEG)
    out[:, K_ID:K_ID + P] = np.eye(P)
    out[:, K_ONE:K_ONE + P] = 1.0
    theta = np.float32(ROPE_THETA)
    for at, rot in ((0, ROT), (ROT // 2, ROT_A)):
        powers = -np.arange(0, rot, 2, dtype=np.float32) / np.float32(rot)
        out[:, K_FREQ + at:K_FREQ + at + rot // 2] = theta ** powers
    return out


class Head:

    def __init__(self, group, h, maps, v_col, mask, chunk):
        self.group, self.h, self.maps, self.v_col, self.mask = group, h, maps, v_col, mask
        self.chunk = chunk


def heads_of(group):
    out = []
    if group == "a":
        for h in range(A_HEADS):
            maps = [((2 * h + j) // 4, 2 + (2 * h + j) // 4, 32 * ((2 * h + j) % 4), 32) for j in (0, 1)]
            out.append(Head(group, h, maps, AV + h * HD, K_CAUSAL, h // 2))
    elif group in "bc":
        q0, k0, v0 = (4, 7, BV) if group == "b" else (10, 13, CV)
        mask = K_DILATED if group == "b" else K_CAUSAL
        for h in range(B_HEADS):
            out.append(Head(group, h, [(q0 + h // 2, k0 + h // 2, 64 * (h % 2), 64)],
                            v0 + h * HD, mask, (2 if group == "b" else 5) + h // 2))
    else:
        for h in range(MEM_HEADS):
            out.append(Head(group, h, [(h // 2, h // 2, 64 * (h % 2), 64)], h * HD, K_ZERO, KC - 2 + h // 2))
    return out


def middle_events(layer):
    def steps(group):
        heads = heads_of(group)
        for i in range(len(heads) + 3):
            out = []
            if i < len(heads):
                out.append(("scores", heads[i]))
            if 0 <= i - 2 < len(heads):
                out.append(("turn", heads[i - 2]))
            if 0 <= i - 3 < len(heads):
                out.append(("apply", heads[i - 3]))
            if 0 <= i - 1 < len(heads):
                out.append(("normalise", heads[i - 1]))
            if group != "a" and 0 <= i - 3 < len(heads) and (i - 3) % 2:
                out.append(("chunk", heads[i - 3]))
            yield out

    a, b, c, m = (steps(g) for g in "abcm")
    ev = []

    def put(*parts):
        for x in parts:
            ev.extend(x if isinstance(x, list) else [x])

    def gain(*chunks):
        return [("mem_gain", kc) for kc in chunks]

    def qk(*pairs):
        return [("turn_qk", p) for p in pairs]

    put(("in", (0, 0)), ("in", (0, 1)), ("in", (0, 2)), ("norm", 1), ("in", (0, 3)), ("in", (1, 0)), ("store_in", 0))
    if layer == 0:
        put(("mem_norm", 0), ("in", (1, 1)), ("angles", 0), ("in", (1, 2)), ("turn_mem", 0), ("turn_mem", 1),
            ("in", (1, 3)), ("tables", 0), ("turn_mem", 2), ("turn_mem", 3), ("in", (2, 0)))
    else:
        put(("in", (1, 1)), ("in", (1, 2)), ("in", (1, 3)), ("in", (2, 0)))
    put(("store_in", 1), ("rotate", "a"), gain(0, 1, 2), ("in", (2, 1)), gain(3, 4, 5, 6, 7), ("in", (2, 2)),
        qk(0, 1), ("in", (2, 3)), next(a), ("in", (3, 0)), ("store_in", 2), next(a))
    for j in range(1, 4):
        put(("in", (3, j)), next(a))
    put(("in", (4, 0)), ("store_in", 3), ("rotate", "b"), next(a), ("in", (4, 1)), next(a), ("in", (4, 2)), qk(2, 3),
        ("in", (4, 3)), next(b), ("in", (5, 0)), ("store_in", 4), qk(4), next(b))
    put(("in", (5, 1)), next(b), ("in", (5, 2)), next(b), ("in", (5, 3)), ("turn_mixed", 0), next(b))
    put(("mem_k", 0), ("store_in", 5), ("rotate", "c"), next(b), ("mem_k", 1), next(b), ("store_k", 0),
        ("out", 0), qk(5, 6), next(b), next(c), ("out", 1), next(b), next(c), ("out", 2), qk(7), next(c),
        ("out", 3), next(c), next(c), ("out", 4), next(c), next(c), ("out", 5), next(c), next(c),
        ("out", 6), ("out", 7))
    put(("residual", 2), ("mem_v", 0), ("mem_q", 0), ("norm", 2), ("mem_q", 1), ("store_q", 0), ("catch_up", 0),
        next(m), next(m), ("mem_v", 1), next(m), ("store_v", 0))
    for x in m:
        put(x)
    put(("mem_o", 0), ("mem_o", 1))
    assert not list(a) + list(b) + list(c)
    return ev


PIECE_EVENTS = ("in", "out", "mem_k", "mem_v", "mem_q", "mem_o")
LAGGING = ("in", "mem_k")
CLOSING = (("out", KC - 1), ("mem_o", 1), ("mem_q", 1))


def number_events():
    count = {"head": 0, "map": 0, "turn_qk": 0}
    layers = []
    for layer in range(DEPTH):
        piece = layer * P_LAYER + P_FFN
        heads, part = {}, []
        events = middle_events(layer)
        for what, arg in events:
            if what == "scores":
                heads[arg.group, arg.h] = {k: count[k] for k in ("head", "map")}
                count["head"] += 1
                count["map"] += len(arg.maps)
        for what, arg in events:
            n = {}
            if what in PIECE_EVENTS:
                n = {"piece": piece}
                piece += 1
            elif what == "catch_up":
                n = {"piece": piece}
            elif what in ("scores", "turn", "apply", "normalise", "chunk"):
                n = heads[arg.group, arg.h]
            elif what in count:
                n = {what: count[what]}
                count[what] += 1
            part.append((what, arg, n))
        assert piece == layer * P_LAYER + P_FFN2
        layers.append(part)
    return layers, count


def decoder_trunk(nc, t, constants, out):
    layers, count = number_events()
    with ExitStack() as ctx:
        def sb(name, shape, dt=F32):
            return ctx.enter_context(nc.sbuf_tensor(name, shape, dt))

        def sem(name):
            return ctx.enter_context(nc.semaphore(name))

        x_cols = sb("x_cols", [P, KC, SEQ])
        w_raw = sb("w_raw", [P, RAW, PIECE])
        w_hi = sb("w_hi", [P, RING, PIECE], F32R)
        w_lo = sb("w_lo", [P, RING, PIECE], F32R)
        c_hi = sb("c_hi", [P, KC, SEQ], F32R)
        c_lo = sb("c_lo", [P, KC, SEQ], F32R)
        mem_cols = sb("mem_cols", [P, KC, MEM])
        m_hi = sb("m_hi", [P, KC, MEM], F32R)
        m_lo = sb("m_lo", [P, KC, MEM], F32R)
        mem_k = sb("mem_k", [P, 2, MEM])
        mem_q = sb("mem_q", [P, 2, SEQ])
        mem_v = sb("mem_v", [P, TT, MEM_HEADS * HD])
        qkv = sb("qkv", [P, TT, 3 * D])
        qk_cols = sb("qk_cols", [P, 16, SEQ])
        mixed = sb("mixed", [P, TT, D])
        x_in = qkv[:, :, 0:D]
        mem_rows = qkv[:, :, 2 * D:3 * D]
        out_rows = qkv[:, :, 0:D]
        squares = mixed[:, :, :].rearrange("p t (k n) -> p (t k) n", n=SEQ)
        probs = sb("probs", [P, PLACES, HALF])
        probs_t = sb("probs_t", [P, 2, HALF])
        bias = sb("bias", [P, PLACES, TT])
        sums = sb("sums", [P, PLACES, TT])
        recips = sb("recips", [P, PLACES, TT])
        out_a = sb("out_a", [P, TT, A_HEADS, HD])
        sq_a = sb("sq_a", [P, TT, A_HEADS, HD])
        rms_a = sb("rms_a", [P, 4, TT * A_HEADS])
        rot_1 = sb("rot_1", [P, TT, 2 * B_HEADS * ROT])
        rot_2 = sb("rot_2", [P, TT, 2 * B_HEADS * ROT])
        gate = sb("gate", [P, HALF])
        hidden = sb("hidden", [P, HALF])
        h_hi = sb("h_hi", [P, HALF], F32R)
        h_lo = sb("h_lo", [P, HALF], F32R)
        last_hi, last_lo = (m[:, 0:2, :].rearrange("p k n -> p (k n)") for m in (m_hi, m_lo))
        rms = sb("rms", [P, 4, TT])
        rms_scaled = sb("rms_scaled", [P, TT])
        diag = sb("diag", [P, TT, P])
        rms_cols = sb("rms_cols", [P, SEQ])
        const = sb("const", [P, K_COLS])
        gain_rows = sb("gain_rows", [10 * KC, P])
        gains = sb("gains", [P, 10 * KC])
        final_gain = qk_cols[:, 0:D // SEQ, :].rearrange("p k n -> p (k n)")
        lambdas = sb("lambdas", [P, 4, DEPTH, A_MAP])
        lam = sb("lam", [P, 4, DEPTH, 2])
        subln = sb("subln", [P, DEPTH, HD])
        pos = sb("pos", [P, TT], I32)
        pos_f = sb("pos_f", [P, TT])
        angle = sb("angle", [P, 4, 2, TT, NF])
        cos_h = sb("cos_h", [P, TT, ROT])
        sin_h = sb("sin_h", [P, TT, ROT])
        cos_a = sb("cos_a", [P, TT, ROT_A])
        sin_a = sb("sin_a", [P, TT, ROT_A])

        ident = const[:, K_ID:K_ID + P]
        bank = [ctx.enter_context(nc.psum_tensor(f"bank{i}", [P, HALF], F32)) for i in range(8)]
        GATE, UP = 4, 5
        MEM_K, MEM_V, MEM_Q, TURN_A = 1, 7, 0, 5
        OUT_BANKS = ((4, 5), (7, 0))

        params_loaded = sem("params_loaded")
        identity_loaded = sem("identity_loaded")
        gains_loaded = sem("gains_loaded")
        x_loaded = [sem(f"x_loaded{i}") for i in range(2)]
        mem_loaded = sem("mem_loaded")
        weights_loaded = [sem(f"weights_loaded{i}") for i in range(RAW)]
        pieces_rounded = sem("pieces_rounded")
        pieces_split = sem("pieces_split")
        pieces_used = sem("pieces_used")
        vector_done = sem("vector_done")
        pool_done = sem("pool_done")
        gains_turned = sem("gains_turned")
        gains_ready = sem("gains_ready")
        lambdas_summed = sem("lambdas_summed")
        lambdas_exp = sem("lambdas_exp")
        angles_ready = sem("angles_ready")
        sines_ready = sem("sines_ready")
        tables_ready = sem("tables_ready")
        mem_squared = sem("mem_squared")
        mem_scaled = sem("mem_scaled")
        mem_turned = sem("mem_turned")
        mem_cols_ready = sem("mem_cols_ready")
        mem_rounded = sem("mem_rounded")
        mem_split = sem("mem_split")
        x_turned = sem("x_turned")
        quarter_done = sem("quarter_done")
        x_updated = sem("x_updated")
        squares_added = sem("squares_added")
        squares_summed = sem("squares_summed")
        x_squared = sem("x_squared")
        rms_ready = sem("rms_ready")
        diag_ready = sem("diag_ready")
        rms_spread = sem("rms_spread")
        rms_cols_ready = sem("rms_cols_ready")
        mixed_turned = sem("mixed_turned")
        cols_rounded = sem("cols_rounded")
        cols_split = sem("cols_split")
        gates_scaled = sem("gates_scaled")
        gates_active = sem("gates_active")
        gates_weighted = sem("gates_weighted")
        hidden_ready = sem("hidden_ready")
        hidden_rounded = sem("hidden_rounded")
        hidden_split = sem("hidden_split")
        rows0_stored = sem("rows0_stored")
        rows1_stored = sem("rows1_stored")
        rotated = sem("rotated")
        qk_turned = sem("qk_turned")
        qk_stored = sem("qk_stored")
        mem_k_stored = sem("mem_k_stored")
        mem_v_stored = sem("mem_v_stored")
        mem_q_stored = sem("mem_q_stored")
        scored = sem("scored")
        masked = sem("masked")
        exped = sem("exped")
        normalised = sem("normalised")
        probs_turned = sem("probs_turned")
        probs_stored = sem("probs_stored")
        applied = sem("applied")
        mixed_stored = sem("mixed_stored")
        final_loaded = sem("final_loaded")
        out_turned = sem("out_turned")
        out_gained = sem("out_gained")
        out0_ready = sem("out0_ready")
        out1_ready = sem("out1_ready")
        out_stored = sem("out_stored")

        def raw(view):
            return view.bitcast(F32)

        def gain_col(layer, which, kc):
            at = (which * DEPTH + layer) * KC + kc
            return gains[:, at:at + 1]

        def kind_of_ffn(f):
            return f // 2, f % 2

        def ffn_piece(f):
            layer, which = kind_of_ffn(f)
            return layer * P_LAYER + which * P_FFN2

        def stage_gain(stage, kc):
            return gain_col(stage // STAGES, (0, 1, 2, 4)[stage % STAGES], kc)

        def last_piece(layer, what, arg):
            return next(n["piece"] for w, a, n in layers[layer] if w == what and a == arg) + 1

        def end_piece(stage):
            layer, which = stage // STAGES, stage % STAGES
            if which == 2:
                return last_piece(layer, "out", KC - 1)
            return layer * P_LAYER + (0, P_FFN, None, P_FFN2)[which]

        def ready_quarter(stage, p):
            if stage == 0:
                return x_turned, p + 1
            if p < 3:
                return quarter_done, 3 * (stage - 1) + p + 1
            return pieces_used, end_piece(stage)

        result = bank[7][:, 0:SEQ]

        def chunk_split(layer, arg):
            first = T_MO - (KC - 2) if arg.group == "m" else T_OUT
            return layer * T_LAYER + first + arg.chunk + 1

        def gain_load(which):
            name = ("ffn1_norm", "mix_norm", "memq_norm", "memkv_norm", "ffn2_norm")[which]
            at = which * DEPTH * KC
            return gain_rows[at:at + DEPTH * KC, :], t[name].rearrange("l (k p) -> (l k) p", p=P)

        owner = {n["map"] + j: n["head"] for part in layers for what, arg, n in part
                 if what == "scores" for j in range(len(arg.maps))}
        place_free = {m: owner[m - PLACES] + 1 for m in owner if m >= PLACES}
        n_heads = count["head"]

        block = ctx.enter_context(nc.Block())

        @block.sync
        def _(sp):
            def load_piece(n, i, source):
                slot = n % RAW
                if n >= RAW:
                    sp.wait_ge(pieces_split, n - RAW + 1 + RING * i)
                sp.dma_start(w_raw[:, slot, :].rearrange("p (k n) -> p k n", n=source.shape[-1]),
                             source).then_inc(weights_loaded[slot], 16)

            def up_source(w, half, i):
                view = w.rearrange("(h k p) f -> p h k f", h=2, p=P)
                return view[:, half, :, bass.ds(i * 256, 256)]

            def down_source(w, half, i):
                view = w.rearrange("(c h p) n -> p c h n", h=2, p=P)
                return view[:, bass.ds(i, 1), half, :]

            def load_ffn(f):
                layer, which = kind_of_ffn(f)
                name = "ffn1" if which == 0 else "ffn2"
                wg, wu, wd = (t[f"{name}_w_{x}"][layer] for x in ("gate", "up", "down"))
                base = ffn_piece(f)

                for j, source in enumerate((up_source(wg, 0, 0), up_source(wg, 1, 0),
                                            up_source(wu, 0, 0), up_source(wu, 1, 0))):
                    load_piece(base + j, 0, source)
                with sp.Fori(0, STEPS - 1) as i:
                    for j, source in enumerate((up_source(wg, 0, i + 1), up_source(wg, 1, i + 1),
                                                up_source(wu, 0, i + 1), up_source(wu, 1, i + 1),
                                                down_source(wd, 0, i), down_source(wd, 1, i))):
                        load_piece(base + 4 + j, i, source)
                load_piece(base + P_FFN - 2, 0, down_source(wd, 0, STEPS - 1))
                load_piece(base + P_FFN - 1, 0, down_source(wd, 1, STEPS - 1))

            def load_middle(layer):
                w_in = t["w_in"][layer].rearrange("(j k p) n -> p j k n", k=2, p=P)
                kv = t["mem_w_kv"][layer].rearrange("(h k p) n -> p h k n", h=2, p=P)
                w_out = t["w_out"][layer].rearrange("(k p) n -> p k n", p=P)
                wq = t["mem_w_q"][layer].rearrange("(h k p) n -> p h k n", h=2, p=P)
                wo = t["mem_w_o"][layer].rearrange("(k p) n -> p k n", p=P)
                for what, arg, n in layers[layer]:
                    if what == "in":
                        b, j = arg
                        load_piece(n["piece"], 0, w_in[:, j, :, b * HALF:(b + 1) * HALF])
                    elif what == "mem_k":
                        load_piece(n["piece"], 0, kv[:, arg, :, 0:256])
                    elif what == "mem_v":
                        load_piece(n["piece"], 0, kv[:, arg, :, 256:512])
                    elif what == "out":
                        load_piece(n["piece"], 0, w_out[:, arg:arg + 1, :])
                    elif what == "mem_q":
                        load_piece(n["piece"], 0, wq[:, arg, :, :])
                    elif what == "mem_o":
                        load_piece(n["piece"], 0, wo[:, arg:arg + 1, :])

            x = t["x"][0].rearrange("(t p) d -> p t d", p=P)
            for half in range(2):
                if half:
                    for which in range(2):
                        sp.dma_start(*gain_load(which)).then_inc(gains_loaded, 16)
                sp.dma_start(x_in[:, :, half * HALF:(half + 1) * HALF],
                             x[:, :, half * HALF:(half + 1) * HALF]).then_inc(x_loaded[half], 16)
            for layer in range(DEPTH):
                load_ffn(2 * layer)
                load_middle(layer)
                load_ffn(2 * layer + 1)
            sp.wait_ge(applied, n_heads)
            sp.dma_start(final_gain, t["final_norm"].partition_broadcast(P)).then_inc(final_loaded, 16)
            for j in range(2 * TT):
                tt, half = 1 - j % 2, j // 2
                sp.wait_ge((out0_ready, out1_ready)[tt], half + 1)
                sp.dma_start(out[0, tt * P:(tt + 1) * P, half * HALF:(half + 1) * HALF],
                             out_rows[:, tt, half * HALF:(half + 1) * HALF]).then_inc(out_stored, 16)
            sp.wait_ge(out_stored, 16 * 2 * TT)

        @block.gpsimd
        def _(pool):
            count = [0]

            def link(ins):
                count[0] += 1
                ins.then_inc(pool_done, 1)
                pool.wait_ge(pool_done, count[0])

            def load(to, source, signal=params_loaded):
                pool.dma_start(to, source).then_inc(signal, 16)

            def add_squares(stage):
                for p in range(4):
                    pair = squares[:, 2 * p:2 * p + 2, :]
                    if stage:
                        pool.wait_ge(x_squared, 4 * stage + p + 1)
                    else:
                        pool.wait_ge(x_updated, p + 1)
                        x = x_cols[:, 2 * p:2 * p + 2, :]
                        pool.tensor_tensor(pair, x, x, ALU.mult).then_inc(x_squared, 1)
                        pool.wait_ge(x_squared, p + 1)
                    add = pool.tensor_tensor(pair[:, 0, :], pair[:, 0, :], pair[:, 1, :], ALU.add)
                    if p % 2:
                        link(add)
                        half = squares[:, 2 * p - 2, :]
                        pool.tensor_tensor(half, half, pair[:, 0, :], ALU.add).then_inc(squares_added, 1)

            add_squares(0)
            load(const[:, 0:K_ID], constants[:, 0:K_ID])
            for tt in range(TT):
                load(pos[:, tt:tt + 1], t["positions"][0, tt * P:(tt + 1) * P].unsqueeze(1))
            for j, name in enumerate(("q1", "k1", "q2", "k2")):
                load(lambdas[:, j, :, :].rearrange("p l d -> p (l d)"),
                     t[f"diff_lambda_{name}"].rearrange("l d -> (l d)").partition_broadcast(P))
            load(subln[:, :, :].rearrange("p l d -> p (l d)"),
                 t["diff_subln"].rearrange("l d -> (l d)").partition_broadcast(P))
            load(mem_rows, t["mem"][0].rearrange("(t p) d -> p t d", p=P), mem_loaded)

            for layer in range(DEPTH):
                if layer:
                    add_squares(STAGES * layer)
                add_squares(STAGES * layer + 1)
                for what, arg, n in layers[layer]:
                    if what == "residual":
                        add_squares(STAGES * layer + 2)
                    if what != "rotate":
                        continue
                    first, heads, wide, rot, cos, sin, blocks = {
                        "a": (AQ, 4 * A_HEADS, A_MAP, ROT_A, cos_a, sin_a, 1),
                        "b": (BQ, 2 * B_HEADS, HD, ROT, cos_h, sin_h, 3),
                        "c": (CQ, 2 * C_HEADS, HD, ROT, cos_h, sin_h, 6)}[arg]
                    if layer == 0 and arg == "a":
                        pool.wait_ge(tables_ready, 1)
                    pool.wait_ge(rows0_stored, layer * BLOCKS + blocks)
                    pool.wait_ge(rows1_stored, layer * BLOCKS + blocks)
                    h = rot // 2
                    for tt in range(TT):
                        rows = qkv[:, tt, first:first + heads * wide].rearrange("p (h d) -> p h d", d=wide)
                        t1, t2 = (r[:, tt, 0:heads * rot].rearrange("p (h d) -> p h d", d=rot) for r in (rot_1, rot_2))
                        c = cos[:, tt, :].unsqueeze(1).broadcast_to([P, heads, rot])
                        s = sin[:, tt, :].unsqueeze(1).broadcast_to([P, heads, rot])
                        pool.tensor_tensor(t1, rows[:, :, 0:rot], c, ALU.mult)
                        pool.tensor_tensor(t2[:, :, 0:h], rows[:, :, h:rot], s[:, :, 0:h], ALU.mult)
                        link(pool.tensor_tensor(t2[:, :, h:rot], rows[:, :, 0:h], s[:, :, h:rot], ALU.mult))
                        last = pool.tensor_tensor(rows[:, :, 0:rot], t1, t2, ALU.add)
                        if tt < TT - 1:
                            link(last)
                    last.then_inc(rotated, 1)
                add_squares(STAGES * layer + 3)
            add_squares(LAST_STAGE)

        @block.scalar
        def _(act):
            def prepare(n, i=0):
                slot = n % RING
                act.wait_ge(weights_loaded[n % RAW], 16 * (n // RAW + 1) + 16 * (RING // RAW) * i)
                if n >= RING:
                    act.wait_ge(pieces_used, n - RING + 1 + RING * i)
                act.activation(w_hi[:, slot, :], w_raw[:, n % RAW, :], ACT.Copy).then_inc(pieces_rounded, 1)

            def ahead(n, count=1, i=0):
                for k in range(count):
                    if RING <= n + k + RING < PIECES:
                        prepare(n + k + RING, i)

            def columns(stage):
                for p in range(4):
                    act.wait_ge(x_updated, 4 * stage + p + 1)
                    if stage < LAST_STAGE:
                        for kc in (2 * p, 2 * p + 1):
                            act.activation(c_hi[:, kc, :], x_cols[:, kc, :], ACT.Copy,
                                           scale=stage_gain(stage, kc)).then_inc(cols_rounded, 1)
                    if stage:
                        act.activation(squares[:, 2 * p:2 * p + 2, :], x_cols[:, 2 * p:2 * p + 2, :],
                                       ACT.Square).then_inc(x_squared, 1)
                    if stage == 0 and p < RAW:
                        prepare(p)

            def ffn(f):
                base = ffn_piece(f)
                s0 = f * STEPS

                def silu(s, i=0):
                    act.wait_ge(gates_scaled, s + 1 + i)
                    act.activation(gate[:, :], gate[:, :], ACT.Silu).then_inc(gates_active, 1)

                def round_hidden(s, i=0, used=None, to=h_hi):
                    act.wait_ge(hidden_ready, s + 1 + i)
                    if used is not None:
                        act.wait_ge(pieces_used, used + RING * i)
                    act.activation(to[:, :], hidden[:, :], ACT.Copy).then_inc(hidden_rounded, 1)

                ahead(base - 2, 4)
                act.wait_ge(rms_spread, f + 1)
                act.activation(rms_cols[:, :], bank[6][:, 0:SEQ], ACT.Copy).then_inc(rms_cols_ready, 1)
                silu(s0)
                ahead(base + 2, 2)
                round_hidden(s0)
                with act.Fori(0, STEPS - 2) as i:
                    n = base + 4
                    ahead(n, 2, i)
                    silu(s0 + 1, i)
                    ahead(n + 2, 4, i)
                    round_hidden(s0 + 1, i, n + 6)
                n = base + 4 + 6 * (STEPS - 2)
                ahead(n, 2)
                silu(s0 + STEPS - 1)
                ahead(n + 2, 2)
                round_hidden(s0 + STEPS - 1, to=last_hi)
                ahead(n + 4, 2)

            def middle(layer):
                done = layer * P_LAYER + P_FFN - 2
                for what, arg, n in layers[layer]:
                    if what == "catch_up" or (what in PIECE_EVENTS and (what, arg) not in CLOSING):
                        ahead(done, n["piece"] - done)
                        done = n["piece"]
                    if what == "store_in":
                        b = arg
                        act.wait_ge(rms_ready, STAGES * layer + 2)
                        act.wait_ge(pieces_used, last_piece(layer, "in", (b, 3)))
                        act.activation(qkv[:, 0, b * HALF:(b + 1) * HALF], bank[(2 * b) % 4][:, :], ACT.Copy,
                                       scale=rms[:, 3, 0:1]).then_inc(rows0_stored, 1)
                        if b in SCALAR_STORES:
                            act.wait_ge(rows1_stored, layer * BLOCKS + b)
                            act.activation(qkv[:, 1, b * HALF:(b + 1) * HALF], bank[(2 * b + 1) % 4][:, :], ACT.Copy,
                                           scale=rms[:, 3, 1:2]).then_inc(rows1_stored, 1)
                    elif what == "store_k":
                        act.wait_ge(pieces_used, last_piece(layer, "mem_k", 1))
                        act.activation(mem_k[:, :, :], bank[MEM_K][:, :].rearrange("p (k n) -> p k n", k=2),
                                       ACT.Copy).then_inc(mem_k_stored, 1)
                    elif what == "store_v":
                        act.wait_ge(pieces_used, last_piece(layer, "mem_v", 1))
                        act.activation(mem_v[:, :, :], bank[MEM_V][:, :].rearrange("p (k n) -> p k n", k=2),
                                       ACT.Copy).then_inc(mem_v_stored, 1)
                    elif what == "store_q":
                        act.wait_ge(pieces_used, last_piece(layer, "mem_q", 1))
                        act.activation(mem_q[:, :, :], bank[MEM_Q][:, :].rearrange("p (k n) -> p k n", k=2),
                                       ACT.Copy).then_inc(mem_q_stored, 1)
                    elif what == "tables":
                        act.wait_ge(angles_ready, 1)
                        act.activation(angle[:, 3, :, :, :], angle[:, 3, :, :, :], ACT.Sin).then_inc(sines_ready, 1)
                        act.wait_ge(lambdas_summed, 1)
                        act.activation(lam[:, 1, :, :], lam[:, 0, :, :], ACT.Exp).then_inc(lambdas_exp, 1)
                    elif what == "mem_norm":
                        act.wait_ge(mem_loaded, 16)
                        for tt in range(TT):
                            act.activation(probs[:, 2 * tt:2 * tt + 2, :].rearrange("p a b -> p (a b)"),
                                           mem_rows[:, tt, :], ACT.Square,
                                           accum_out=rms_a[:, 0, tt:tt + 1]).then_inc(mem_squared, 1)
                    elif what == "turn_mem":
                        act.wait_ge(mem_turned, arg + 1)
                        act.activation(mem_cols[:, 2 * arg:2 * arg + 2, :],
                                       bank[4 + arg % 2][:, :].rearrange("p (k n) -> p k n", k=2),
                                       ACT.Copy).then_inc(mem_cols_ready, 1)
                    elif what == "mem_gain":
                        if arg == 0:
                            act.wait_ge(mem_cols_ready, 4)
                        act.activation(m_hi[:, arg, :], mem_cols[:, arg, :], ACT.Copy,
                                       scale=gain_col(layer, 3, arg)).then_inc(mem_rounded, 1)
                    elif what == "turn_qk":
                        act.wait_ge(qk_turned, n["turn_qk"] + 1)
                        act.activation(qk_cols[:, 2 * arg:2 * arg + 2, :],
                                       bank[4 + n["turn_qk"] % 2][:, :].rearrange("p (k n) -> p k n", k=2),
                                       ACT.Copy).then_inc(qk_stored, 1)
                    elif what == "turn_mixed":
                        act.wait_ge(mixed_turned, layer + 1)
                        act.activation(c_hi[:, 0:2, :], bank[TURN_A][:, :].rearrange("p (k n) -> p k n", k=2),
                                       ACT.Copy).then_inc(cols_rounded, 2)
                    elif what == "chunk":
                        last_use = ("mem_q", 1) if arg.group == "m" else ("in", (BLOCKS - 1, 3))
                        act.wait_ge(pieces_used, last_piece(layer, *last_use))
                        act.wait_ge(applied, n["head"] + 1)
                        act.activation(c_hi[:, arg.chunk, :], result, ACT.Copy).then_inc(cols_rounded, 1)
                    elif what == "residual":
                        columns(STAGES * layer + arg)
                    elif what == "scores":
                        for j in range(len(arg.maps)):
                            m = n["map"] + j
                            wide = (128, 256) if arg.group != "m" else (256, 256)
                            act.wait_ge(masked, m + 1)
                            at = 0
                            for tt in range(TT):
                                view = probs[:, m % PLACES, at:at + wide[tt]]
                                total = sums[:, m % PLACES, tt:tt + 1]
                                last = act.activation(view, view, ACT.Exp, scale=-1.0,
                                                      bias=bias[:, m % PLACES, tt:tt + 1], accum_out=total)
                                at += wide[tt]
                            last.then_inc(exped, 1)

            act.dma_start(const[:, K_ID:K_COLS], constants[:, K_ID:K_COLS]).then_inc(identity_loaded, 16)
            for which in range(2, 5):
                act.dma_start(*gain_load(which)).then_inc(gains_loaded, 16)
            act.wait_ge(gains_turned, 1)
            act.activation(gains[:, :], bank[7][:, 0:10 * KC], ACT.Copy).then_inc(gains_ready, 1)
            act.wait_ge(gains_ready, 1)
            columns(0)
            for n in range(RAW, RING):
                prepare(n)

            for layer in range(DEPTH):
                if layer:
                    columns(STAGES * layer)
                ffn(2 * layer)
                columns(STAGES * layer + 1)
                middle(layer)
                columns(STAGES * layer + 3)
                ffn(2 * layer + 1)
            columns(LAST_STAGE)
            act.wait_ge(out_gained, 1)
            act.wait_ge(rms_ready, LAST_STAGE + 1)
            for half in range(2):
                at = slice(half * HALF, (half + 1) * HALF)
                act.activation(out_rows[:, 0, at], out_rows[:, 0, at], ACT.Copy,
                               scale=rms[:, 3, 0:1]).then_inc(out0_ready, 1)

        @block.vector
        def _(dve):
            count = [0]

            def link(ins):
                count[0] += 1
                ins.then_inc(vector_done, 1)
                dve.wait_ge(vector_done, count[0])

            def prepare(n, i=0):
                slot = n % RING
                dve.wait_ge(pieces_rounded, n + 1 + RING * i)
                dve.tensor_tensor(w_lo[:, slot, :], w_raw[:, n % RAW, :], raw(w_hi[:, slot, :]),
                                  ALU.subtract).then_inc(pieces_split, 1)

            def ahead(n, count=1, i=0):
                for k in range(count):
                    if RING <= n + k + RING < PIECES:
                        prepare(n + k + RING, i)

            def rsqrt(y, source, total, tmp, width, final):
                link(dve.tensor_scalar(total, source, 1.0 / width, EPS, ALU.mult, ALU.add))
                link(dve.tensor_scalar(y.bitcast(I32), total.bitcast(I32), -0.5, float(0x5F3759DF),
                                       ALU.mult, ALU.add))
                for k in range(3):
                    link(dve.scalar_tensor_tensor(tmp, y, -0.5, y, ALU.mult, ALU.mult))
                    link(dve.tensor_tensor(tmp, tmp, total, ALU.mult))
                    last = dve.scalar_tensor_tensor(y, tmp, 1.5, y, ALU.add, ALU.mult)
                    if k < 2 or final is None:
                        link(last)
                    else:
                        last.then_inc(final, 1)

            def norm(stage):
                dve.wait_ge(squares_summed, stage + 1)
                rsqrt(rms[:, 3, :], bank[6][:, 0:TT], rms[:, 0, :], rms[:, 2, :], D, rms_ready)
                dve.wait_ge(rms_ready, stage + 1)

            def spread(f):
                dve.tensor_scalar(diag[:, 0, :], ident, rms[:, 3, 0:1], None, ALU.mult)
                dve.tensor_scalar(diag[:, 1, :], ident, rms[:, 3, 1:2], None, ALU.mult).then_inc(diag_ready, 1)

            def residual(stage, first=None):
                for p in range(5):
                    if p < 4:
                        dve.wait_ge(*ready_quarter(stage, p))
                        x = x_cols[:, 2 * p:2 * p + 2, :]
                        b = bank[p][:, :].rearrange("p (k n) -> p k n", k=2)
                        if stage:
                            dve.tensor_tensor(x, b, x, ALU.add).then_inc(x_updated, 1)
                        else:
                            dve.tensor_copy(x, b).then_inc(x_updated, 1)
                    if p and first is not None:
                        q = p - 1
                        dve.wait_ge(x_updated, 4 * stage + q + 1)
                        if stage == 0 and q == 0:
                            dve.wait_ge(gains_ready, 1)
                        for k in (2 * q, 2 * q + 1):
                            dve.wait_ge(cols_rounded, first + k + 1)
                            dve.scalar_tensor_tensor(c_lo[:, k, :], x_cols[:, k, :], stage_gain(stage, k),
                                                     raw(c_hi[:, k, :]), ALU.mult,
                                                     ALU.subtract).then_inc(cols_split, 1)
                        if stage == 0 and q < RAW:
                            prepare(q)

            def ffn(f):
                base = ffn_piece(f)
                s0 = f * STEPS

                def scale_gate(s, used, i=0):
                    dve.wait_ge(pieces_used, used + RING * i)
                    dve.tensor_tensor(gate[:, :].rearrange("p (c n) -> p c n", c=2),
                                      bank[GATE][:, :].rearrange("p (c n) -> p c n", c=2),
                                      rms_cols[:, :].unsqueeze(1).broadcast_to([P, 2, SEQ]),
                                      ALU.mult).then_inc(gates_scaled, 1)

                def multiply(s, used, i=0):
                    dve.wait_ge(gates_active, s + 1 + i)
                    dve.scalar_tensor_tensor(gate[:, :].rearrange("p (c n) -> p c n", c=2),
                                             gate[:, :].rearrange("p (c n) -> p c n", c=2), 0.5,
                                             rms_cols[:, :].unsqueeze(1).broadcast_to([P, 2, SEQ]),
                                             ALU.mult, ALU.mult).then_inc(gates_weighted, 1)
                    dve.wait_ge(pieces_used, used + RING * i)
                    dve.wait_ge(gates_weighted, s + 1 + i)
                    dve.tensor_tensor(hidden[:, :], bank[UP][:, :], gate[:, :], ALU.mult).then_inc(hidden_ready, 1)

                def split_hidden(s, i=0, hi=h_hi, lo=h_lo):
                    dve.wait_ge(hidden_rounded, s + 1 + i)
                    dve.tensor_tensor(lo[:, :], hidden[:, :], raw(hi[:, :]),
                                      ALU.subtract).then_inc(hidden_split, 1)

                ahead(base - 2, 2)
                norm(f // 2 * STAGES + f % 2 * 3)
                spread(f)
                ahead(base, 1)
                dve.wait_ge(rms_cols_ready, f + 1)
                scale_gate(s0, base + 2)
                ahead(base + 1, 2)
                multiply(s0, base + 4)
                ahead(base + 3, 1)
                split_hidden(s0)
                with dve.Fori(0, STEPS - 2) as i:
                    n = base + 4
                    scale_gate(s0 + 1, n + 2, i)
                    ahead(n, 3, i)
                    multiply(s0 + 1, n + 4, i)
                    ahead(n + 3, 3, i)
                    split_hidden(s0 + 1, i)
                n = base + 4 + 6 * (STEPS - 2)
                scale_gate(s0 + STEPS - 1, n + 2)
                ahead(n, 3)
                multiply(s0 + STEPS - 1, n + 4)
                ahead(n + 3, 1)
                split_hidden(s0 + STEPS - 1, hi=last_hi, lo=last_lo)
                ahead(n + 4, 2)

            def finish_a(layer):
                b = bank[7][:, :].rearrange("p (t h d) -> p t h d", t=TT, h=A_HEADS)
                link(dve.tensor_copy(out_a[:, :, :, :], b))
                link(dve.tensor_tensor(sq_a[:, :, :, :], out_a[:, :, :, :], out_a[:, :, :, :], ALU.mult))
                link(dve.tensor_reduce(rms_a[:, 0, :], sq_a[:, :, :, :].rearrange("p t h d -> p (t h) d"),
                                       AX.X, ALU.add))
                rsqrt(rms_a[:, 3, :], rms_a[:, 0, :], rms_a[:, 0, :], rms_a[:, 2, :], HD, None)
                flat = out_a[:, :, :, :].rearrange("p t h d -> p (t h) d")
                factor = rms_a[:, 3, :].unsqueeze(2).broadcast_to([P, TT * A_HEADS, HD])
                link(dve.tensor_tensor(flat, flat, factor, ALU.mult))
                g = subln[:, layer, :].unsqueeze(1).broadcast_to([P, A_HEADS, HD])
                for tt in range(TT):
                    last = dve.tensor_tensor(mixed[:, tt, 0:A_HEADS * HD].rearrange("p (h d) -> p h d", d=HD),
                                             out_a[:, tt, :, :], g, ALU.mult)
                last.then_inc(mixed_stored, 1)

            def middle(layer):
                done = layer * P_LAYER + P_FFN - 2
                for what, arg, n in layers[layer]:
                    if what == "catch_up" or (what in PIECE_EVENTS and (what, arg) not in CLOSING):
                        to = n["piece"] - (what in LAGGING)
                        ahead(done, to - done)
                        done = to
                    if what == "store_in" and arg not in SCALAR_STORES:
                        b = arg
                        if b - 1 in SCALAR_STORES:
                            dve.wait_ge(rows1_stored, layer * BLOCKS + b)
                        dve.wait_ge(pieces_used, last_piece(layer, "in", (b, 3)))
                        dve.tensor_scalar(qkv[:, 1, b * HALF:(b + 1) * HALF], bank[(2 * b + 1) % 4][:, :],
                                          rms[:, 3, 1:2], None, ALU.mult).then_inc(rows1_stored, 1)
                    elif what == "angles":
                        angles()
                    elif what == "tables":
                        tables()
                    elif what == "mem_norm":
                        dve.wait_ge(mem_squared, TT)
                        rsqrt(rms_a[:, 3, 0:TT], rms_a[:, 0, 0:TT], rms_a[:, 0, 0:TT], rms_a[:, 2, 0:TT], D, None)
                        for tt in range(TT):
                            last = dve.tensor_scalar(mem_rows[:, tt, :], mem_rows[:, tt, :], rms_a[:, 3, tt:tt + 1],
                                                     None, ALU.mult)
                        last.then_inc(mem_scaled, 1)
                    elif what == "mem_gain":
                        dve.wait_ge(mem_rounded, layer * KC + arg + 1)
                        dve.scalar_tensor_tensor(m_lo[:, arg, :], mem_cols[:, arg, :], gain_col(layer, 3, arg),
                                                 raw(m_hi[:, arg, :]), ALU.mult, ALU.subtract).then_inc(mem_split, 1)
                    elif what == "norm":
                        norm(STAGES * layer + arg)
                        if arg == 2:
                            link(dve.tensor_scalar(rms_scaled[:, :], rms[:, 3, :], -HD ** -0.5, None, ALU.mult))
                    elif what == "residual":
                        residual(STAGES * layer + arg, layer * T_LAYER + T_MQ)
                    elif what == "turn_mixed":
                        dve.wait_ge(cols_rounded, layer * T_LAYER + T_OUT + 2)
                        b = bank[TURN_A][:, :].rearrange("p (k n) -> p k n", k=2)
                        dve.tensor_tensor(c_lo[:, 0:2, :], b, raw(c_hi[:, 0:2, :]),
                                          ALU.subtract).then_inc(cols_split, 2)
                    elif what == "chunk":
                        dve.wait_ge(cols_rounded, chunk_split(layer, arg))
                        dve.tensor_tensor(c_lo[:, arg.chunk, :], result, raw(c_hi[:, arg.chunk, :]),
                                          ALU.subtract).then_inc(cols_split, 1)
                    elif what == "scores":
                        for j in range(len(arg.maps)):
                            m = n["map"] + j
                            dve.wait_ge(scored, m + 1)
                            if m >= PLACES:
                                dve.wait_ge(probs_turned, place_free[m])
                            wide = (128, 256) if arg.group != "m" else (256, 256)
                            at = 0
                            for tt in range(TT):
                                if arg.group == "m":
                                    mask, scale = const[:, K_ZERO:K_ZERO + 256], rms_scaled[:, tt:tt + 1]
                                else:
                                    mask = const[:, arg.mask + at:arg.mask + at + wide[tt]]
                                    scale = -(len(arg.maps) / HD) ** 0.5
                                last = dve.tensor_tensor_reduce(
                                    probs[:, m % PLACES, at:at + wide[tt]], bank[4 + m % 2][:, at:at + wide[tt]], mask,
                                    scale, BIG, ALU.add, ALU.min, bias[:, m % PLACES, tt:tt + 1])
                                at += wide[tt]
                            last.then_inc(masked, 1)
                    elif what == "turn":
                        h = n["head"]
                        dve.wait_ge(probs_turned, h + 1)
                        if h >= 2:
                            dve.wait_ge(applied, h - 1)
                        wide = 384 if arg.group != "m" else 512
                        dve.tensor_copy(probs_t[:, h % 2, 0:wide], bank[6][:, 0:wide]).then_inc(probs_stored, 1)
                    elif what == "normalise" and arg.group == "a":
                        combine(n, layer)
                    elif what == "normalise":
                        normalise(arg, n)
                    elif what == "apply" and arg.group == "a" and arg.h == A_HEADS - 1:
                        dve.wait_ge(applied, n["head"] + 1)
                        finish_a(layer)

            def combine(n, layer):
                a = n["map"] % PLACES
                dve.wait_ge(exped, n["map"] + 2)
                link(dve.reciprocal(recips[:, a:a + 2, :], sums[:, a:a + 2, :]))
                link(dve.tensor_scalar(recips[:, a + 1, :], recips[:, a + 1, :], lam[:, 3, layer, 0:1], None, ALU.mult))
                for tt, at in enumerate((slice(0, 128), slice(128, 384))):
                    p1, p2 = probs[:, a, at], probs[:, a + 1, at]
                    link(dve.tensor_scalar(p2, p2, recips[:, a + 1, tt:tt + 1], None, ALU.mult))
                    last = dve.scalar_tensor_tensor(p1, p1, recips[:, a, tt:tt + 1], p2, ALU.mult, ALU.add)
                last.then_inc(normalised, 1)

            def normalise(arg, n):
                a = n["map"] % PLACES
                dve.wait_ge(exped, n["map"] + 1)
                link(dve.reciprocal(recips[:, a, :], sums[:, a, :]))
                split = 256 if arg.group == "m" else 128
                for tt, at in enumerate((slice(0, split), slice(split, split + 256))):
                    last = dve.tensor_scalar(probs[:, a, at], probs[:, a, at], recips[:, a, tt:tt + 1], None, ALU.mult)
                last.then_inc(normalised, 1)

            def angles():
                dve.wait_ge(params_loaded, 16 * N_PARAMS)
                link(dve.tensor_copy(pos_f[:, :], pos[:, :]))
                freq = const[:, K_FREQ:K_FREQ + NF]
                for tt in range(TT):
                    for part in range(2):
                        last = dve.tensor_scalar(angle[:, 0, part, tt, :], freq, pos_f[:, tt:tt + 1], None, ALU.mult)
                link(last)
                magic = 1.5 * 2.0 ** 23
                for part in range(2):
                    link(dve.tensor_scalar(angle[:, 1, part, :, :], angle[:, 0, part, :, :], 1 / (2 * math.pi),
                                           0.25 * part, ALU.mult, ALU.add))
                link(dve.tensor_scalar(angle[:, 1, :, :, :], angle[:, 1, :, :, :], magic, None, ALU.add))
                link(dve.tensor_scalar(angle[:, 1, :, :, :], angle[:, 1, :, :, :], -magic, None, ALU.add))
                c1 = 6.28125
                c2 = float(np.float32(round((2 * math.pi - c1) * 2 ** 20) / 2 ** 20))
                c3 = 2 * math.pi - c1 - c2
                source = angle[:, 0, :, :, :]
                for c in (c1, c2, c3):
                    link(dve.scalar_tensor_tensor(angle[:, 3, :, :, :].rearrange("p a t f -> p (a t f)"),
                                                  angle[:, 1, :, :, :].rearrange("p a t f -> p (a t f)"), -c,
                                                  source.rearrange("p a t f -> p (a t f)"), ALU.mult, ALU.add))
                    source = angle[:, 3, :, :, :]
                link(dve.tensor_scalar(angle[:, 3, 1, :, :], angle[:, 3, 1, :, :], math.pi / 2, None, ALU.add))
                dve.tensor_scalar(angle[:, 3, :, :, :], angle[:, 3, :, :, :], 3.1415925, -3.1415925,
                                  ALU.min, ALU.max).then_inc(angles_ready, 1)
                for j in range(2):
                    link(dve.tensor_tensor(lambdas[:, 2 * j, :, :], lambdas[:, 2 * j, :, :],
                                           lambdas[:, 2 * j + 1, :, :], ALU.mult))
                    last = dve.tensor_reduce(lam[:, 0, j, :], lambdas[:, 2 * j, :, :], AX.X, ALU.add)
                    if j == 0:
                        link(last)
                last.then_inc(lambdas_summed, 1)
                for layer in range(DEPTH):
                    init = 0.8 - 0.6 * math.exp(-0.3 * layer)
                    link(dve.tensor_scalar(subln[:, layer, :], subln[:, layer, :], 1.0 - init, None, ALU.mult))

            def tables():
                dve.wait_ge(lambdas_exp, 1)
                for layer in range(DEPTH):
                    init = 0.8 - 0.6 * math.exp(-0.3 * layer)
                    link(dve.tensor_tensor(lam[:, 2, layer, 0:1], lam[:, 1, 1, layer:layer + 1],
                                           lam[:, 1, 0, layer:layer + 1], ALU.subtract))
                    link(dve.tensor_scalar(lam[:, 3, layer, 0:1], lam[:, 2, layer, 0:1], -init, None, ALU.add))
                dve.wait_ge(sines_ready, 1)
                for part, (head, small) in enumerate(((sin_h, sin_a), (cos_h, cos_a))):
                    for table, at, n in ((head, 0, ROT // 2), (small, ROT // 2, ROT_A // 2)):
                        value = angle[:, 3, part, :, at:at + n]
                        dve.tensor_scalar(table[:, :, 0:n], value, 1.0 if part else -1.0, None, ALU.mult)
                        last = dve.tensor_copy(table[:, :, n:2 * n], value)
                last.then_inc(tables_ready, 1)

            residual(0, 0)
            for n in range(RAW, RING):
                prepare(n)

            for layer in range(DEPTH):
                if layer:
                    residual(STAGES * layer, layer * T_LAYER + T_FFN1)
                ffn(2 * layer)
                residual(STAGES * layer + 1, layer * T_LAYER + T_MIX)
                middle(layer)
                residual(STAGES * layer + 3, layer * T_LAYER + T_FFN2)
                ffn(2 * layer + 1)
            residual(LAST_STAGE)
            dve.wait_ge(final_loaded, 16)
            for half in range(2):
                dve.wait_ge(out_turned, half + 1)
                at = slice(half * HALF, (half + 1) * HALF)
                for tt in range(TT):
                    last = dve.tensor_tensor(out_rows[:, tt, at], bank[OUT_BANKS[tt][half]][:, :], final_gain[:, at],
                                             ALU.mult)
            last.then_inc(out_gained, 1)
            norm(LAST_STAGE)
            dve.wait_ge(out_gained, 1)
            for half in range(2):
                at = slice(half * HALF, (half + 1) * HALF)
                dve.tensor_scalar(out_rows[:, 1, at], out_rows[:, 1, at], rms[:, 3, 1:2], None,
                                  ALU.mult).then_inc(out1_ready, 1)

        @block.tensor
        def _(pe):
            reader = {}

            def claim(b):
                if b in reader:
                    pe.wait_ge(*reader[b])

            def three(out_, lhs, rhs, start, stop):
                (lh, ll), (rh, rl) = lhs, rhs
                pe.matmul(out_, lh, rh, start=start, stop=False, skip_group_check=True)
                pe.matmul(out_, ll, rh, start=False, stop=False, skip_group_check=True)
                return pe.matmul(out_, lh, rl, start=False, stop=stop, skip_group_check=True)

            def w(slot, a, b):
                return w_hi[:, slot, a:b], w_lo[:, slot, a:b]

            def col(kc, a, b):
                return c_hi[:, kc, a:b], c_lo[:, kc, a:b]

            def signal(ins, c, closing):
                if c == KC - 1:
                    ins.then_inc(pieces_used, 1)
                elif closing and c % 2:
                    ins.then_inc(quarter_done, 1)

            def sum_squares(stage):
                pe.wait_ge(squares_added, 2 * stage + 2)
                claim(6)
                for tt in range(TT):
                    for half in range(2):
                        last = pe.matmul(bank[6][:, tt:tt + 1], squares[:, 4 * half, tt * P:(tt + 1) * P],
                                         const[:, K_ONE:K_ONE + 1], start=half == 0, stop=half == 1)
                last.then_inc(squares_summed, 1)
                reader[6] = (rms_ready, stage + 1)

            def updates(stage):
                for b in range(4):
                    reader[b] = (x_updated, 4 * stage + b + 1)

            def ffn(f, cols_at):
                base = ffn_piece(f)
                s0 = f * STEPS

                def columns(n, b, i=0, wait_cols=False, after=None):
                    for half in range(2):
                        slot = (n + half) % RING
                        pe.wait_ge(pieces_split, n + half + 1 + RING * i)
                        for k in range(4):
                            kc = 4 * half + k
                            if wait_cols:
                                pe.wait_ge(cols_split, cols_at + kc + 1)
                            for fc in range(2):
                                at = k * 256 + fc * P
                                last = three(bank[b][:, fc * 256:(fc + 1) * 256], w(slot, at, at + P),
                                             col(kc, 0, SEQ), start=(kc == 0 and fc == 0),
                                             stop=(kc == KC - 1))
                            if after and kc in after:
                                after[kc]()
                        last.then_inc(pieces_used, 1)

                def spread():
                    pe.wait_ge(diag_ready, f + 1)
                    claim(6)
                    for tt in range(TT):
                        last = pe.matmul(bank[6][:, tt * P:(tt + 1) * P], const[:, K_ONE:K_ONE + P], diag[:, tt, :],
                                         start=True, stop=True)
                    last.then_inc(rms_spread, 1)
                    reader[6] = (rms_cols_ready, f + 1)

                def down(n, s, first, final, i=0, hi=h_hi, lo=h_lo):
                    pe.wait_ge(hidden_split, s + 1 + i)
                    if first:
                        for b in range(4):
                            claim(b)
                    for half in range(2):
                        slot = (n + half) % RING
                        pe.wait_ge(pieces_split, n + half + 1 + RING * i)
                        for c in range(KC):
                            at = c % 2 * SEQ
                            last = three(bank[c // 2][:, at:at + SEQ], w(slot, c * P, (c + 1) * P),
                                         (hi[:, half * SEQ:(half + 1) * SEQ], lo[:, half * SEQ:(half + 1) * SEQ]),
                                         start=first and half == 0 and c % 2 == 0, stop=final and half == 1)
                            signal(last, c, final and half == 1)

                claim(GATE)
                columns(base, GATE, wait_cols=True)
                claim(UP)
                columns(base + 2, UP, after={0: lambda: sum_squares(f // 2 * STAGES + f % 2 * 3), 5: spread})
                pe.wait_ge(gates_scaled, s0 + 1)
                columns(base + 4, GATE)
                pe.wait_ge(hidden_ready, s0 + 1)
                columns(base + 6, UP)
                down(base + 8, s0, True, False)
                with pe.Fori(0, STEPS - 2) as i:
                    n = base + 10
                    pe.wait_ge(gates_scaled, s0 + 2 + i)
                    columns(n, GATE, i)
                    pe.wait_ge(hidden_ready, s0 + 2 + i)
                    columns(n + 2, UP, i)
                    down(n + 4, s0 + 1, False, False, i)
                down(base + P_FFN - 2, s0 + STEPS - 1, False, True, hi=last_hi, lo=last_lo)
                reader[GATE] = (gates_scaled, s0 + STEPS)
                reader[UP] = (hidden_ready, s0 + STEPS)

            def half_product(n, half, b, lhs, rhs, ready):
                pe.wait_ge(pieces_split, n + 1)
                for k in range(4):
                    kc = 4 * half + k
                    pe.wait_ge(*ready(kc))
                    for j in range(2):
                        last = three(bank[b][:, j * 256:(j + 1) * 256], lhs(k, kc, j), rhs(k, kc, j),
                                     start=(kc == 0 and j == 0), stop=(kc == KC - 1))
                last.then_inc(pieces_used, 1)

            def full_product(n, kc, first, final):
                pe.wait_ge(pieces_split, n + 1)
                for c in range(KC):
                    if first and c % 2 == 0:
                        claim(c // 2)
                    at = c % 2 * SEQ
                    last = three(bank[c // 2][:, at:at + SEQ], w(n % RING, c * P, (c + 1) * P), col(kc, 0, SEQ),
                                 start=first and c % 2 == 0, stop=final)
                    signal(last, c, final)

            def middle(layer):
                c0 = layer * T_LAYER
                for what, arg, n in layers[layer]:
                    if what == "in":
                        b, j = arg
                        piece = n["piece"]
                        pe.wait_ge(pieces_split, piece + 1)
                        for k in range(2):
                            if b == 0:
                                pe.wait_ge(cols_split, c0 + T_MIX + 2 * j + k + 1)
                            for tt in range(TT):
                                if j == 0 and k == 0:
                                    claim((2 * b + tt) % 4)
                                last = three(bank[(2 * b + tt) % 4][:, :], col(2 * j + k, tt * P, (tt + 1) * P),
                                             w(piece % RING, k * HALF, (k + 1) * HALF),
                                             start=(j == 0 and k == 0), stop=(j == 3 and k == 1))
                        last.then_inc(pieces_used, 1)
                        if j == 3:
                            reader[(2 * b) % 4] = (rows0_stored, layer * BLOCKS + b + 1)
                            reader[(2 * b + 1) % 4] = (rows1_stored, layer * BLOCKS + b + 1)
                    elif what == "norm":
                        sum_squares(STAGES * layer + arg)
                    elif what == "turn_mem":
                        b = 4 + arg % 2
                        pe.wait_ge(mem_scaled, 1)
                        claim(b)
                        for k in range(2):
                            for tt in range(TT):
                                at = k * 256 + tt * P
                                last = pe.transpose(bank[b][:, at:at + P],
                                                    mem_rows[:, tt, (2 * arg + k) * P:(2 * arg + k + 1) * P], ident)
                        last.then_inc(mem_turned, 1)
                        reader[b] = (mem_cols_ready, arg + 1)
                    elif what == "mem_k":
                        slot = n["piece"] % RING
                        if arg == 0:
                            claim(MEM_K)
                        half_product(n["piece"], arg, MEM_K,
                                     lambda k, kc, j: w(slot, k * 256 + j * P, k * 256 + (j + 1) * P),
                                     lambda k, kc, j: (m_hi[:, kc, :], m_lo[:, kc, :]),
                                     lambda kc: (mem_split, layer * KC + kc + 1))
                        reader[MEM_K] = (mem_k_stored, layer + 1)
                    elif what == "mem_v":
                        slot = n["piece"] % RING
                        if arg == 0:
                            claim(7)
                        half_product(n["piece"], arg, MEM_V,
                                     lambda k, kc, j: (m_hi[:, kc, j * P:(j + 1) * P], m_lo[:, kc, j * P:(j + 1) * P]),
                                     lambda k, kc, j: w(slot, k * 256, (k + 1) * 256),
                                     lambda kc: (mem_split, layer * KC + kc + 1))
                        reader[7] = (mem_v_stored, layer + 1)
                    elif what == "mem_q":
                        slot = n["piece"] % RING
                        if arg == 0:
                            claim(MEM_Q)
                        half_product(n["piece"], arg, MEM_Q,
                                     lambda k, kc, j: w(slot, k * 256 + j * P, k * 256 + (j + 1) * P),
                                     lambda k, kc, j: col(kc, 0, SEQ),
                                     lambda kc: (cols_split, c0 + T_MQ + kc + 1))
                        reader[MEM_Q] = (mem_q_stored, layer + 1)
                    elif what == "out":
                        pe.wait_ge(cols_split, c0 + T_OUT + max(arg, 1) + 1)
                        full_product(n["piece"], arg, arg == 0, arg == KC - 1)
                    elif what == "mem_o":
                        pe.wait_ge(cols_split, c0 + T_MO + arg + 1)
                        full_product(n["piece"], KC - 2 + arg, arg == 0, arg == 1)
                    elif what == "residual":
                        updates(STAGES * layer + arg)
                    elif what == "turn_mixed":
                        pe.wait_ge(mixed_stored, layer + 1)
                        claim(TURN_A)
                        for k in range(2):
                            for tt in range(TT):
                                at = k * 256 + tt * P
                                last = pe.transpose(bank[TURN_A][:, at:at + P], mixed[:, tt, k * P:(k + 1) * P], ident)
                        last.then_inc(mixed_turned, 1)
                        reader[TURN_A] = (cols_split, c0 + T_OUT + 2)
                    elif what == "turn_qk":
                        pe.wait_ge(rotated, layer * 3 + {0: 1, 1: 1, 2: 2, 3: 2, 4: 2}.get(arg, 3))
                        b = 4 + n["turn_qk"] % 2
                        claim(b)
                        for k in range(2):
                            blk = 2 * arg + k
                            first = blk * P if blk < 4 else (BQ + (blk - 4) * P if blk < 10 else CQ + (blk - 10) * P)
                            for tt in range(TT):
                                at = k * 256 + tt * P
                                last = pe.transpose(bank[b][:, at:at + P], qkv[:, tt, first:first + P], ident)
                        last.then_inc(qk_turned, 1)
                        reader[b] = (qk_stored, n["turn_qk"] + 1)
                    elif what == "scores":
                        mem = arg.group == "m"
                        if mem and arg.h == 0:
                            pe.wait_ge(mem_q_stored, layer + 1)
                            pe.wait_ge(mem_k_stored, layer + 1)
                        elif not mem:
                            pe.wait_ge(qk_stored, layer * 8 + max(kb for _, kb, _, _ in arg.maps) // 2 + 1)
                        for j, (qb, kb, p0, ps) in enumerate(arg.maps):
                            m = n["map"] + j
                            b = 4 + m % 2
                            claim(b)
                            at = 0
                            for tt in range(TT):
                                keys = 256 if mem else (tt + 1) * P
                                q, k = (mem_q, mem_k) if mem else (qk_cols, qk_cols)
                                last = pe.matmul(bank[b][:, at:at + keys], q[p0:p0 + ps, qb, tt * P:(tt + 1) * P],
                                                 k[p0:p0 + ps, kb, 0:keys], start=True, stop=True)
                                at += keys
                            last.then_inc(scored, 1)
                            reader[b] = (masked, m + 1)
                    elif what == "turn":
                        h, m = n["head"], n["map"]
                        pe.wait_ge(normalised, h + 1)
                        claim(6)
                        for k in range(4 if arg.group == "m" else 3):
                            to = k // 2 + 2 * (k % 2) if arg.group == "m" else k
                            last = pe.transpose(bank[6][:, to * P:(to + 1) * P],
                                                probs[:, m % PLACES, k * P:(k + 1) * P], ident)
                        last.then_inc(probs_turned, 1)
                        reader[6] = (probs_stored, h + 1)
                    elif what == "apply":
                        h = n["head"]
                        pe.wait_ge(probs_stored, h + 1)
                        if arg.group == "m":
                            pe.wait_ge(mem_v_stored, layer + 1)
                        elif arg.h == 0:
                            stored = layer * BLOCKS + {"a": 2, "b": 4, "c": 6}[arg.group]
                            pe.wait_ge(rows0_stored, stored)
                            pe.wait_ge(rows1_stored, stored)
                        if arg.group == "a":
                            if arg.h == 0:
                                claim(7)
                            for tt in range(TT):
                                at = (tt * A_HEADS + arg.h) * HD
                                terms = [(0, 0)] if tt == 0 else [(1, 0), (2, 1)]
                                for k, (blk, vt) in enumerate(terms):
                                    last = pe.matmul(bank[7][:, at:at + HD], probs_t[:, h % 2, blk * P:(blk + 1) * P],
                                                     qkv[:, vt, arg.v_col:arg.v_col + HD],
                                                     start=k == 0, stop=k == len(terms) - 1)
                            last.then_inc(applied, 1)
                            if arg.h == A_HEADS - 1:
                                reader[7] = (mixed_stored, layer + 1)
                        else:
                            if arg.h % 2 == 0:
                                claim(7)
                            p0 = HD * (arg.h % 2)
                            to = result[p0:p0 + HD, :]
                            v = mem_v if arg.group == "m" else qkv
                            pe.matmul(to, v[:, 0, arg.v_col:arg.v_col + HD], probs_t[:, h % 2, 0:SEQ],
                                      start=True, stop=False, skip_group_check=True)
                            late = 0 if arg.group == "m" else P
                            pe.matmul(to[:, late:SEQ], v[:, 1, arg.v_col:arg.v_col + HD],
                                      probs_t[:, h % 2, SEQ:2 * SEQ - late],
                                      start=False, stop=True, skip_group_check=True).then_inc(applied, 1)
                            reader[7] = (cols_split, chunk_split(layer, arg))

            pe.wait_ge(identity_loaded, 16)
            for p in range(4):
                if p == 2:
                    pe.wait_ge(gains_loaded, 16 * N_GAINS)
                    pe.transpose(bank[7][:, 0:10 * KC], gain_rows[:, :], const[0:10 * KC, K_ID:K_ID + 10 * KC])\
                      .then_inc(gains_turned, 1)
                    reader[7] = (gains_ready, 1)
                pe.wait_ge(x_loaded[p // 2], 16)
                for k in range(2):
                    for tt in range(TT):
                        at = k * 256 + tt * P
                        last = pe.transpose(bank[p][:, at:at + P], x_in[:, tt, (2 * p + k) * P:(2 * p + k + 1) * P],
                                            ident)
                last.then_inc(x_turned, 1)
            updates(0)
            for layer in range(DEPTH):
                ffn(2 * layer, layer * T_LAYER + T_FFN1)
                updates(STAGES * layer + 1)
                middle(layer)
                updates(STAGES * layer + 3)
                ffn(2 * layer + 1, layer * T_LAYER + T_FFN2)
                updates(STAGES * layer + 4)
            for half in range(2):
                for tt in range(TT):
                    claim(OUT_BANKS[tt][half])
                for k in range(4):
                    c = 4 * half + k
                    if k % 2 == 0:
                        pe.wait_ge(x_updated, 4 * LAST_STAGE + c // 2 + 1)
                    for tt in range(TT):
                        last = pe.transpose(bank[OUT_BANKS[tt][half]][:, k * P:(k + 1) * P],
                                            x_cols[:, c, tt * P:(tt + 1) * P], ident)
                last.then_inc(out_turned, 1)
            sum_squares(LAST_STAGE)


_INS = ["x", "mem", "positions", "ffn1_norm", "ffn1_w_gate", "ffn1_w_up", "ffn1_w_down", "mix_norm", "w_in", "w_out",
        "diff_lambda_q1", "diff_lambda_k1", "diff_lambda_q2", "diff_lambda_k2", "diff_subln", "memq_norm",
        "memkv_norm", "mem_w_q", "mem_w_kv", "mem_w_o", "ffn2_norm", "ffn2_w_gate", "ffn2_w_up", "ffn2_w_down",
        "final_norm"]


def kernel(**inputs):
    import concourse.bacc as bacc
    from concourse.bass_utils import run_bass_kernel_spmd

    nc = bacc.Bacc("TRN2", target_bir_lowering=False, num_devices=1)
    arrays, t = {}, {}

    def add(name, a):
        arrays[f"in_{name}_dram"] = a
        return nc.dram_tensor(f"in_{name}_dram", a.shape, mybir.dt.from_np(a.dtype), kind="ExternalInput").ap()

    for name in _INS:
        t[name] = add(name, np.ascontiguousarray(inputs[name]))
    constants = add("shape_constants", shape_constants())
    out = nc.dram_tensor("out_0_dram", (1, SEQ, D), F32, kind="ExternalOutput").ap()
    decoder_trunk(nc, t, constants, out)
    r = run_bass_kernel_spmd(nc, [arrays], core_ids=[0])
    return r.results[0]["out_0_dram"]
```
